# Optimizing a Trainium2 kernel written in Bass

```python
import jax, jax.numpy as jnp
from jax import lax
import numpy as np

D_MODEL = 1024
BATCH = 1
SEQ = 512
DEPTH = 2

CHUNK = 128
A_GROUPS = 4
A_GROUP_DIM = 128
A_WIDTH = A_GROUPS * A_GROUP_DIM
DIL_WINDOWS = (128, 512, 2048)
DIL_RATES = (1, 4, 16)
N_DIL = 3
B_HEADS = 8
B_HEAD_DIM = 64
B_WIDTH = B_HEADS * B_HEAD_DIM
ROPE_DIM = B_HEAD_DIM // 4
ROPE_THETA = 500000.0
C_WIDTH = 512
C_KERNEL = 31
D_WIDTH = 512
D_KERNEL = 3
D_FF = -(-8 * D_MODEL // (3 * 256)) * 256
EPS = 1e-6
NEG_INF = -1e30

AB_IN = 2 * A_WIDTH + 3 * N_DIL * B_HEADS * B_HEAD_DIM
AB_OUT = A_WIDTH + B_WIDTH
CD_IN = 2 * C_WIDTH + 3 * D_WIDTH
CD_OUT = C_WIDTH + D_WIDTH
N_AB = (DEPTH + 1) // 2
N_CD = DEPTH // 2

kernel_name = 'hybrid_gmlp_dilattn_conformer_shortconv'

def rms_norm(x, g):
    xf = x.astype(jnp.float32)
    y = xf * lax.rsqrt(jnp.mean(xf * xf, axis=-1, keepdims=True) + EPS)
    return (y * g.astype(jnp.float32)).astype(x.dtype)

def layer_norm(x, g, b):
    xf = x.astype(jnp.float32)
    xc = xf - jnp.mean(xf, axis=-1, keepdims=True)
    y = xc * lax.rsqrt(jnp.mean(xc * xc, axis=-1, keepdims=True) + EPS)
    return (y * g.astype(jnp.float32) + b.astype(jnp.float32)).astype(x.dtype)

def apply_rope(x, pos):
    half = ROPE_DIM // 2
    inv_freq = ROPE_THETA ** (-jnp.arange(half, dtype=jnp.float32) * 2.0 / ROPE_DIM)
    ang = pos[:, None] * inv_freq[None, :]
    cos = jnp.cos(ang)[None, :, None, :]
    sin = jnp.sin(ang)[None, :, None, :]
    xf = x.astype(jnp.float32)
    x1 = xf[..., :half]
    x2 = xf[..., half:ROPE_DIM]
    out = jnp.concatenate([x1 * cos - x2 * sin, x1 * sin + x2 * cos, xf[..., ROPE_DIM:]], axis=-1)
    return out.astype(x.dtype)

def causal_depthwise_conv(x, w):
    k, c = w.shape
    return lax.conv_general_dilated(
        x, w.astype(x.dtype)[:, None, :], window_strides=(1,), padding=[(k - 1, 0)],
        dimension_numbers=('NWC', 'WIO', 'NWC'), feature_group_count=c)

def chunked_spatial_gating(u, v, w_s, b_s):
    bn, s, _ = u.shape
    nc = s // CHUNK
    vg = v.reshape(bn, nc, CHUNK, A_GROUPS, A_GROUP_DIM)
    causal = jnp.tril(jnp.ones((CHUNK, CHUNK), dtype=bool))
    w = jnp.where(causal[None], w_s, 0.0).astype(v.dtype)
    mixed = jnp.einsum('gts,bnsgc->bntgc', w, vg) + b_s.T.astype(v.dtype)[None, None, :, :, None]
    return u * mixed.reshape(bn, s, A_WIDTH)

def dilated_group_attention(q, k, v, rate, n_back):
    bn, s, h, dh = q.shape
    span = rate * n_back
    s_pad = -(-s // span) * span
    length = s_pad // rate
    nb = length // n_back

    def to_blocks(t):
        t = jnp.pad(t, ((0, 0), (0, s_pad - s), (0, 0), (0, 0)))
        t = t.reshape(bn, length, rate, h, dh).transpose(0, 2, 1, 3, 4)
        return t.reshape(bn, rate, nb, n_back, h, dh)

    def with_prev(t):
        prev = jnp.pad(t[:, :, :-1], ((0, 0), (0, 0), (1, 0), (0, 0), (0, 0), (0, 0)))
        return jnp.concatenate([prev, t], axis=3)

    qb = to_blocks(q)
    kk = with_prev(to_blocks(k))
    vv = with_prev(to_blocks(v))
    scores = jnp.einsum('brnqhd,brnkhd->brnhqk', qb.astype(jnp.float32),
                        kk.astype(jnp.float32)) * (dh ** -0.5)
    qi = jnp.arange(n_back)[:, None]
    kj = jnp.arange(2 * n_back)[None, :]
    dist = qi + n_back - kj
    band = (dist >= 0) & (dist <= n_back)
    exists = (jnp.arange(nb)[:, None, None] > 0) | (kj[None] >= n_back)
    mask = band[None] & exists
    scores = jnp.where(mask[None, None, :, None], scores, NEG_INF)
    lse = jax.nn.logsumexp(scores, axis=-1)
    probs = jnp.exp(scores - lse[..., None])
    out = jnp.einsum('brnhqk,brnkhd->brnqhd', probs, vv.astype(jnp.float32))
    out = out.reshape(bn, rate, length, h, dh).transpose(0, 2, 1, 3, 4).reshape(bn, s_pad, h, dh)[:, :s]
    lse = lse.transpose(0, 1, 2, 4, 3).reshape(bn, rate, length, h)
    lse = lse.transpose(0, 2, 1, 3).reshape(bn, s_pad, h)[:, :s]
    return out, lse

def mixer_ab(h, w_in, sgu_g, sgu_b, sgu_w, sgu_bias, q_g, k_g, w_out):
    bn, s, _ = h.shape
    proj = h @ w_in
    a = jax.nn.gelu(proj[..., :2 * A_WIDTH], approximate=False)
    u, v = a[..., :A_WIDTH], a[..., A_WIDTH:]
    a_out = chunked_spatial_gating(u, layer_norm(v, sgu_g, sgu_b), sgu_w, sgu_bias)
    qkv = proj[..., 2 * A_WIDTH:].reshape(bn, s, 3, N_DIL, B_HEADS, B_HEAD_DIM)
    pos = jnp.arange(s, dtype=jnp.float32)
    outs, lses = [], []
    for g in range(N_DIL):
        q = apply_rope(rms_norm(qkv[:, :, 0, g], q_g[g]), pos)
        k = apply_rope(rms_norm(qkv[:, :, 1, g], k_g[g]), pos)
        o, l = dilated_group_attention(q, k, qkv[:, :, 2, g], DIL_RATES[g], DIL_WINDOWS[g] // DIL_RATES[g])
        outs.append(o)
        lses.append(l)
    wts = jax.nn.softmax(jnp.stack(lses), axis=0)
    b_out = jnp.sum(wts[..., None] * jnp.stack(outs), axis=0).astype(h.dtype).reshape(bn, s, B_WIDTH)
    return jnp.concatenate([a_out, b_out], axis=-1) @ w_out

def mixer_cd(h, w_in, conv_c_w, conv_c_b, c_ln_g, c_ln_b, conv_d_w, w_out):
    proj = h @ w_in
    c = proj[..., :C_WIDTH] * jax.nn.sigmoid(proj[..., C_WIDTH:2 * C_WIDTH])
    c = causal_depthwise_conv(c, conv_c_w) + conv_c_b.astype(c.dtype)
    c = jax.nn.silu(layer_norm(c, c_ln_g, c_ln_b))
    gate_b, gate_c, hv = jnp.split(proj[..., 2 * C_WIDTH:], 3, axis=-1)
    d = gate_b * causal_depthwise_conv(gate_c * hv, conv_d_w)
    return jnp.concatenate([c, d], axis=-1) @ w_out

def swiglu(h, w_gate, w_up, w_down):
    return (jax.nn.silu(h @ w_gate) * (h @ w_up)) @ w_down

def setup_inputs(seed: int = 0) -> dict:
    key = jax.random.key(seed)
    ks = jax.random.split(key, 24)
    f32 = jnp.float32

    def nrm(k, shape, scale):
        return jax.random.normal(k, shape, f32) * scale

    def gain(k, shape):
        return 1.0 + 0.05 * jax.random.normal(k, shape, f32)

    return {
        'x': jax.random.normal(ks[0], (BATCH, SEQ, D_MODEL), f32),
        'ab_norm_g': gain(ks[1], (N_AB, D_MODEL)),
        'ab_w_in': nrm(ks[2], (N_AB, D_MODEL, AB_IN), D_MODEL ** -0.5),
        'sgu_norm_g': gain(ks[3], (N_AB, A_WIDTH)),
        'sgu_norm_b': nrm(ks[4], (N_AB, A_WIDTH), 0.02),
        'sgu_w': nrm(ks[5], (N_AB, A_GROUPS, CHUNK, CHUNK), 0.5 * CHUNK ** -0.5),
        'sgu_bias': gain(ks[6], (N_AB, A_GROUPS, CHUNK)),
        'q_norm_g': gain(ks[7], (N_AB, N_DIL, B_HEAD_DIM)),
        'k_norm_g': gain(ks[8], (N_AB, N_DIL, B_HEAD_DIM)),
        'ab_w_out': nrm(ks[9], (N_AB, AB_OUT, D_MODEL), AB_OUT ** -0.5),
        'cd_norm_g': gain(ks[10], (N_CD, D_MODEL)),
        'cd_w_in': nrm(ks[11], (N_CD, D_MODEL, CD_IN), D_MODEL ** -0.5),
        'conv_c_w': nrm(ks[12], (N_CD, C_KERNEL, C_WIDTH), C_KERNEL ** -0.5),
        'conv_c_b': nrm(ks[13], (N_CD, C_WIDTH), 0.02),
        'c_ln_g': gain(ks[14], (N_CD, C_WIDTH)),
        'c_ln_b': nrm(ks[15], (N_CD, C_WIDTH), 0.02),
        'conv_d_w': nrm(ks[16], (N_CD, D_KERNEL, D_WIDTH), D_KERNEL ** -0.5),
        'cd_w_out': nrm(ks[17], (N_CD, CD_OUT, D_MODEL), CD_OUT ** -0.5),
        'ffn_norm_g': gain(ks[18], (DEPTH, D_MODEL)),
        'ffn_w_gate': nrm(ks[19], (DEPTH, D_MODEL, D_FF), D_MODEL ** -0.5),
        'ffn_w_up': nrm(ks[20], (DEPTH, D_MODEL, D_FF), D_MODEL ** -0.5),
        'ffn_w_down': nrm(ks[21], (DEPTH, D_FF, D_MODEL), D_FF ** -0.5),
    }

def reference(x, ab_norm_g, ab_w_in, sgu_norm_g, sgu_norm_b, sgu_w, sgu_bias, q_norm_g, k_norm_g,
              ab_w_out, cd_norm_g, cd_w_in, conv_c_w, conv_c_b, c_ln_g, c_ln_b, conv_d_w, cd_w_out,
              ffn_norm_g, ffn_w_gate, ffn_w_up, ffn_w_down):
    for layer in range(DEPTH):
        i = layer // 2
        if layer % 2 == 0:
            h = rms_norm(x, ab_norm_g[i])
            x = x + mixer_ab(h, ab_w_in[i], sgu_norm_g[i], sgu_norm_b[i], sgu_w[i], sgu_bias[i],
                             q_norm_g[i], k_norm_g[i], ab_w_out[i])
        else:
            h = rms_norm(x, cd_norm_g[i])
            x = x + mixer_cd(h, cd_w_in[i], conv_c_w[i], conv_c_b[i], c_ln_g[i], c_ln_b[i],
                             conv_d_w[i], cd_w_out[i])
        h = rms_norm(x, ffn_norm_g[layer])
        x = x + swiglu(h, ffn_w_gate[layer], ffn_w_up[layer], ffn_w_down[layer])
    return x


_drawn_inputs = setup_inputs


def setup_inputs(seed=0):
    import zlib

    import numpy as np

    out = dict(_drawn_inputs(seed))
    spreads = {}
    factors = {'sgu_norm_g': 5.646,
     'sgu_norm_b': 26.966,
     'q_norm_g': 8.0,
     'k_norm_g': 8.0,
     'conv_c_b': 4.637,
     'c_ln_g': 3.362,
     'c_ln_b': 8.0,
     'sgu_bias': 3.072}
    for name, (base, spread) in spreads.items():
        noise = np.random.default_rng([zlib.crc32(name.encode()), seed]).standard_normal(out[name].shape)
        drawn = base * np.exp(spread * noise) if base else spread * noise
        out[name] = __import__('jax').numpy.asarray(drawn.astype(out[name].dtype))
    for name, factor in factors.items():
        out[name] = (out[name] * factor).astype(out[name].dtype)
    return out
```

```python
from contextlib import ExitStack

import concourse.bass as bass
from concourse import mybir

F32 = mybir.dt.float32
F32R = mybir.dt.float32r
I32 = mybir.dt.int32
ALU = mybir.AluOpType
ACT = mybir.ActivationFunctionType

P = 128
T = 512
D = 1024
KD = D // P
FF = 2816
NF = FF // P
TB = T // P
HALF = NF // 2
PAIRS = 4
NB_SLOTS = 9
A_SLOTS = 8
AB_SLOTS = A_SLOTS + NB_SLOTS * PAIRS + NB_SLOTS
GU_SLOTS = 2 * NF
DN_SLOTS = 2 * KD
CD_SLOTS = 20
CDO_SLOTS = 8
C_TAPS = 31
D_TAPS = 3
KEYS = T + 2 * P
EPS = 1e-6
MAGIC = 1597463007.0
BIG = 3.0e38

S_PAIR = A_SLOTS
S_FFN0 = AB_SLOTS
S_DN0 = S_FFN0 + GU_SLOTS
S_CD = S_DN0 + DN_SLOTS
S_FFN1 = S_CD + CD_SLOTS + CDO_SLOTS
S_DN1 = S_FFN1 + GU_SLOTS

V_QK = 0
V_AB, V_F0, V_CD, V_F1 = 6, 14, 22, 30
V_CW = 38
V_CB = V_CW + 4 * C_TAPS
V_LG = V_CB + 4
V_LB = V_LG + 4
V_DW = V_LB + 4
V_N = V_DW + 4 * D_TAPS
C_ID = 0
C_HM = 128
C_1024 = 130
C_512 = 131
C_AVG = 132
C_N = C_AVG + 128

MISC = 2
SC = 3
PT = 5
OB = 7
STAT, BC = 7, 6


def build(nc, x_cls, x_nat, w_ab, w_dn0, w_cd, w_dn1, vecs_d, consts_d, rows_d, sguw_d, masks_d, rope_d, out):
    with ExitStack() as ctx:
        def alloc(c, name, shape, dt=F32):
            return c.enter_context(nc.sbuf_tensor(name, shape, dt))

        def sem(name):
            return ctx.enter_context(nc.semaphore(name))

        xres = alloc(ctx, "xres", [P, KD, T])
        xg_hi = alloc(ctx, "xg_hi", [P, KD, T], F32R)
        xg_lo = alloc(ctx, "xg_lo", [P, KD, T], F32R)
        raw = alloc(ctx, "raw", [P, 4 * HALF * P])
        split = alloc(ctx, "split", [P, 48 * P], F32R)
        rstd_b = alloc(ctx, "rstd_b", [P, T])
        sq_acc = alloc(ctx, "sq_acc", [P, T])
        sq_buf = alloc(ctx, "sq_buf", [P, 2, T])
        tmp = alloc(ctx, "tmp", [P, 2, T])
        vecs = alloc(ctx, "vecs", [P, V_N])
        consts = alloc(ctx, "consts", [P, C_N])
        rstd_t = alloc(ctx, "rstd_t", [P, TB])
        rstd_t2 = alloc(ctx, "rstd_t2", [P, TB])
        st_m = alloc(ctx, "st_m", [P, 16])
        st_y = alloc(ctx, "st_y", [P, 16])
        st_t = alloc(ctx, "st_t", [P, 16])
        st_h = alloc(ctx, "st_h", [P, 16])
        nmax = alloc(ctx, "nmax", [P, 2])
        den = alloc(ctx, "den", [P, 2])
        rden = alloc(ctx, "rden", [P, 2])
        gate_cell = alloc(ctx, "gate_cell", [P, 1])
        ident = consts[:, C_ID:C_ID + P]

        with ExitStack() as ab:
            cat_hi = alloc(ab, "cat_hi", [P, KD, T], F32R)
            cat_lo = alloc(ab, "cat_lo", [P, KD, T], F32R)
            rope = alloc(ab, "rope", [P, 2, T])
            qk_next = alloc(ab, "qk_next", [P, 6, T])
            qk_cur = alloc(ab, "qk_cur", [P, 6, T])
            v_raw = alloc(ab, "v_raw", [P, 3, T])
            wide = alloc(ab, "wide", [P, 2 * T])
            with ExitStack() as a:
                vg = alloc(a, "vg", [P, 4, T])
                u = alloc(a, "u", [P, 4, T])
                sguw = alloc(a, "sguw", [P, 4, P])
                rows = alloc(a, "rows", [P, 3, T])
                bn = alloc(a, "bn", [P, TB, 6])
                mv = alloc(a, "mv", [P, TB, 2])
            with ExitStack() as b:
                masks = alloc(b, "masks", [P, TB, KEYS])
                sm = alloc(b, "sm", [P, KEYS])
                prob = alloc(b, "prob", [P, KEYS])
                prob_t = alloc(b, "prob_t", [P, KEYS])
                v_cur = alloc(b, "v_cur", [P, 3, TB, P])
        with ExitStack() as ffn:
            h_hi = alloc(ffn, "h_hi", [P, NF, T], F32R)
            h_lo = alloc(ffn, "h_lo", [P, NF, T], F32R)
            g_act = alloc(ffn, "g_act", [P, 2, T])
        with ExitStack() as cd:
            ccat_hi = alloc(cd, "ccat_hi", [P, KD, T], F32R)
            ccat_lo = alloc(cd, "ccat_lo", [P, KD, T], F32R)
            c_in = alloc(cd, "c_in", [P, 4, T])
            c_acc = alloc(cd, "c_acc", [P, 4, T])
            c_gate = alloc(cd, "c_gate", [P, 2, T])
            c_sig = alloc(cd, "c_sig", [P, 2, T])
            d_y = alloc(cd, "d_y", [P, 2, T])
            d_z = alloc(cd, "d_z", [P, 2, T])
            d_out = alloc(cd, "d_out", [P, 2, T])
            prods = alloc(cd, "prods", [P, 3, T])

        ps = ctx.enter_context(nc.psum_tensor("ps", [P, 8, T], F32))
        scores = ps[:, SC:SC + 2, :].rearrange("p b t -> p (b t)")[:, 0:KEYS]
        probsT = ps[:, PT:PT + 2, :].rearrange("p b t -> p (b t)")[:, 0:KEYS]

        x_loaded = [sem(f"x_loaded_{k}") for k in range(KD)]
        vecs_loaded, xnat_loaded, const_loaded, a_loaded, rope_loaded, masks_loaded = (
            sem(n) for n in ("vecs_loaded", "xnat_loaded", "const_loaded", "a_loaded", "rope_loaded", "masks_loaded"))
        raw3 = [sem(f"raw3_{i}") for i in range(3)]
        raw4 = [sem(f"raw4_{i}") for i in range(4)]
        hi_ready, lo_ready, slot_done = sem("hi_ready"), sem("lo_ready"), sem("slot_done")
        dve = sem("dve")
        xh_ready, xg_ready, sq_ready, sq_used = sem("xh_ready"), sem("xg_ready"), sem("sq_ready"), sem("sq_used")
        stat_ready, rstd_tok, bc_ready, rstd_ready = (
            sem(n) for n in ("stat_ready", "rstd_tok", "bc_ready", "rstd_ready"))
        a_lin, gelu_done, sguw_masked, vt_ready, ln_ready, mix_ready, cat_f, cat_h, cat_l = (
            sem(n) for n in ("a_lin", "gelu_done", "sguw_masked", "vt_ready", "ln_ready", "mix_ready",
                             "cat_f", "cat_h", "cat_l"))
        qkv_used, qk_cur_ready = sem("qkv_used"), sem("qk_cur_ready")
        scores_ready, scores_used, exp_done, probs_ready, pt_ready, pt_out, pv_done = (
            sem(n) for n in ("scores_ready", "scores_used", "exp_done", "probs_ready", "pt_ready", "pt_out",
                             "pv_done"))
        misc_ready, misc_used, rq_ready = sem("misc_ready"), sem("misc_used"), sem("rq_ready")
        out_ready, out_used = sem("out_ready"), sem("out_used")
        up_used, lin_ready, silu_done, h_f, h_h, h_ready, dn_used = (
            sem(n) for n in ("up_used", "lin_ready", "silu_done", "h_f", "h_h", "h_ready", "dn_used"))
        cd_used, cgate_act, ccat_f, ccat_h, ccat_l, conv, mean_ready, xc_ready = (
            sem(n) for n in ("cd_used", "cgate_act", "ccat_f", "ccat_h", "ccat_l", "conv", "mean_ready", "xc_ready"))
        c_ready, prod_ready, prod_added = sem("c_ready"), sem("prod_ready"), sem("prod_added")
        cn_ready, csilu_done, cdo_ready, stored = (
            sem(n) for n in ("cn_ready", "csilu_done", "cdo_ready", "stored"))

        def raw_ab(s):
            return raw[:, (s % 3) * KD * P:(s % 3 + 1) * KD * P]

        def raw_late(q, tiles):
            return raw[:, (q % 4) * HALF * P:((q % 4) * HALF + tiles) * P]

        def hi_lo_ab(s):
            o = (s % 3) * 16 * P
            return split[:, o:o + KD * P], split[:, o + KD * P:o + 2 * KD * P]

        def hi_lo_late(q, tiles):
            o = (q % 2) * 22 * P
            return split[:, o:o + tiles * P], split[:, o + tiles * P:o + 2 * tiles * P]

        def natural(ap):
            return ap.rearrange("p (i r) -> p r i", r=TB)

        def classes(ap):
            return ap.rearrange("p (r i) -> p r i", r=TB)

        block = ctx.enter_context(nc.Block())

        @block.sync
        def _(sp):
            def load(dst, src, s_):
                sp.dma_start(dst, src).then_inc(s_, 16)

            def slot(dram, index, dst, s_):
                load(dst, dram[index, :, :] if isinstance(index, int) else
                     dram[bass.ds(index, 1), :, :].rearrange("a p n -> p (a n)"), s_)

            slot(w_ab, 0, raw_ab(0), raw3[0])
            load(vecs[:], vecs_d, vecs_loaded)
            for k in range(KD):
                load(xres[:, k, :], x_cls[:, k, :], x_loaded[k])
                if k in (3, 7):
                    s = k // 4 + 1
                    slot(w_ab, s, raw_ab(s), raw3[s])
            load(consts[:], consts_d, const_loaded)
            load(sguw[:], sguw_d, a_loaded)
            load(rows[:], rows_d, a_loaded)
            load(rope[:], rope_d, rope_loaded)
            with sp.Fori(1, 6) as i:
                for b in range(3):
                    sp.wait_ge(lo_ready, 3 * i + (b - 2))
                    slot(w_ab, 3 * i + b, raw_ab(b), raw3[b])
            sp.wait_ge(xg_ready, KD)
            sp.wait_ge(sq_used, KD)
            load(xres[:], x_nat, xnat_loaded)
            sp.wait_ge(cat_l, 4)
            load(masks[:], masks_d, masks_loaded)
            with sp.Fori(6, 17) as i:
                for b in range(3):
                    sp.wait_ge(lo_ready, 3 * i + (b - 2))
                    slot(w_ab, 3 * i + b, raw_ab(b), raw3[b])
            for s in (51, 52):
                sp.wait_ge(lo_ready, s - 2)
                slot(w_ab, s, raw_ab(s), raw3[s % 3])

            def phase(dram, start, n, tiles, at, skip=0):
                with sp.Fori(skip, n // 4) as i:
                    for b in range(4):
                        sp.wait_ge(lo_ready, 4 * i + (start + b - 3))
                        slot(dram, 4 * i + (at + b), raw_late(b, tiles), raw4[b])

            sp.wait_ge(lo_ready, AB_SLOTS)
            for b in range(4):
                slot(w_ab, AB_SLOTS + b, raw_late(b, KD), raw4[b])
            phase(w_ab, S_FFN0, GU_SLOTS, KD, AB_SLOTS, skip=1)
            phase(w_dn0, S_DN0, DN_SLOTS, HALF, 0)
            phase(w_cd, S_CD, CD_SLOTS + CDO_SLOTS + GU_SLOTS, KD, 0)
            phase(w_dn1, S_DN1, DN_SLOTS, HALF, 0)
            with sp.Fori(0, KD) as n:
                sp.wait_ge(dn_used, n + (KD + 1))
                sp.dma_start(out[bass.ds(n, 1), :, :].rearrange("a p t -> p (a t)"),
                             xres[:, bass.ds(n, 1), :].rearrange("p a t -> p (a t)")).then_inc(stored, 16)
            sp.wait_ge(stored, 16 * KD)

        @block.gpsimd
        def _(pool):
            pool.wait_ge(a_loaded, 32)
            pool.affine_select(out=sguw[:], in_=sguw[:], compare_op=ALU.is_ge, fill=0.0, base=0,
                               pattern=[[0, 4], [1, P]], channel_multiplier=-1).then_inc(sguw_masked, 1)

            def lo_part(s, src, hi_lo):
                hi, lo = hi_lo
                pool.wait_ge(hi_ready, s + 1)
                pool.tensor_tensor(lo, src, hi.bitcast(F32), ALU.subtract).then_inc(lo_ready, 1)

            with pool.Fori(0, 17) as i:
                for b in range(3):
                    lo_part(3 * i + b, raw_ab(b), hi_lo_ab(b))
            for s in (51, 52):
                lo_part(s, raw_ab(s), hi_lo_ab(s))
            def lo_phase(start, n, tiles):
                with pool.Fori(0, n // 4) as i:
                    for b in range(4):
                        lo_part(4 * i + (start + b), raw_late(b, tiles), hi_lo_late(b, tiles))

            lo_phase(S_FFN0, GU_SLOTS, KD)
            lo_phase(S_DN0, DN_SLOTS, HALF)
            d = 1
            for q in range(20):
                lo_part(S_CD + q, raw_late(q, KD), hi_lo_late(q, KD))
                for _ in range(2 if q >= 3 else 0):
                    if d < C_TAPS:
                        pool.wait_ge(prod_ready, d + 1)
                        if d > 1:
                            pool.wait_ge(prod_added, d - 1)
                        pool.tensor_tensor(c_acc[:, 0, d:T], c_acc[:, 0, d:T], prods[:, d % 3, 0:T - d], ALU.add)\
                            .then_inc(prod_added, 1)
                        d += 1
            assert d == C_TAPS
            lo_phase(S_CD + 20, CDO_SLOTS + GU_SLOTS, KD)
            lo_phase(S_DN1, DN_SLOTS, HALF)

        @block.scalar
        def _(act):
            def hi_late(s, q, tiles, fills):
                act.wait_ge(raw4[q % 4], fills)
                act.wait_ge(slot_done, s - 1)
                act.activation(hi_lo_late(q, tiles)[0], raw_late(q, tiles), ACT.Copy).then_inc(hi_ready, 1)

            def x_hi(k, col):
                gain = vecs[:, col + k:col + k + 1]
                act.activation(xg_hi[:, k, :], xres[:, k, :], ACT.Identity, scale=gain).then_inc(xh_ready, 1)

            def x_square(k, h, m):
                if m >= 2:
                    act.wait_ge(sq_used, m - 1)
                act.activation(sq_buf[:, h, :], xres[:, k, :], ACT.Square).then_inc(sq_ready, 1)

            def first_hi(s):
                act.wait_ge(raw3[s], 16)
                act.activation(hi_lo_ab(s)[0], raw_ab(s), ACT.Copy).then_inc(hi_ready, 1)

            first_hi(0)
            act.wait_ge(vecs_loaded, 16)
            for k in range(KD):
                act.wait_ge(x_loaded[k], 16)
                x_hi(k, V_AB)
                if k == 4:
                    first_hi(1)
            for k in range(KD):
                x_square(k, k % 2, k)
            for j in range(A_SLOTS):
                s = j + 2
                act.wait_ge(raw3[s % 3], 16 * (s // 3 + 1))
                if s >= 3:
                    act.wait_ge(slot_done, s - 2)
                act.activation(hi_lo_ab(s)[0], raw_ab(s), ACT.Copy).then_inc(hi_ready, 1)
                act.wait_ge(a_lin, j + 1)
                dst = vg[:, j, :] if j < 4 else u[:, j - 4, :]
                act.activation(natural(dst), classes(tmp[:, j % 2, :]), ACT.Gelu).then_inc(gelu_done, 1)

            def attention_softmax(j, n):
                act.wait_ge(scores_used, n + 1)
                act.activation(prob[:], sm[:], ACT.Exp, bias=nmax[:, j % 2:j % 2 + 1], scale=-1.0,
                               accum_out=den[:, j % 2:j % 2 + 1]).then_inc(exp_done, 1)

            def probs_out(j, n):
                act.wait_ge(pt_ready, n + 1)
                if j:
                    act.wait_ge(pv_done, n)
                act.activation(prob_t[:], probsT, ACT.Copy).then_inc(pt_out, 1)

            def concat_hi(index, f_count, src):
                act.wait_ge(cat_f, f_count)
                act.activation(cat_hi[:, index, :] if isinstance(index, int) else
                               cat_hi[:, bass.ds(index, 1), :].rearrange("p a t -> p (a t)"),
                               src, ACT.Copy).then_inc(cat_h, 1)

            def pair_stage(st, attn, proj=True):
                for j in range(NB_SLOTS):
                    n = 8 * (st - 1) + j
                    s = S_PAIR + 9 * st + j
                    if attn and j >= 1:
                        probs_out(j - 1, n - 1)
                    if attn and j < 8:
                        attention_softmax(j, n)
                    if not (isinstance(st, int) and s + 2 >= AB_SLOTS):
                        act.wait_ge(raw3[(j + 1) % 3], 16 * (3 * st + (S_PAIR + j + 2) // 3 + 1))
                        act.wait_ge(slot_done, s)
                        act.activation(hi_lo_ab(j + 1)[0], raw_ab(j + 1), ACT.Copy).then_inc(hi_ready, 1)
                    if proj:
                        if not attn and j == 6:
                            for g in range(4):
                                concat_hi(g, g + 1, tmp[:, g % 2, :])
                        act.wait_ge(slot_done, s + 1)
                        bank = MISC if j == 8 else j % 2
                        if j < 6:
                            if attn:
                                act.wait_ge(qk_cur_ready, 6 * st)
                            act.activation(qk_next[:, j, :], ps[:, bank, :], ACT.Copy)
                            if j >= 2:
                                act.wait_ge(misc_ready, misc_ssq(st, j // 2 - 1, attn))
                            elif attn:
                                act.wait_ge(misc_ready, misc_base(st, attn))
                            else:
                                act.wait_ge(sq_used, KD)
                            act.activation(sq_buf[:, j % 2, :], ps[:, bank, :], ACT.Square).then_inc(qkv_used, 1)
                        else:
                            if j == 6 and attn:
                                act.wait_ge(misc_ready, misc_base(st, attn) + 3)
                            act.activation(v_raw[:, j - 6, :], ps[:, bank, :], ACT.Copy).then_inc(qkv_used, 1)
                if attn:
                    concat_hi(st + 3, 4 + st, tmp[:, 0, :])

            pair_stage(0, False)
            with act.Fori(1, PAIRS) as st:
                pair_stage(st, True)
            pair_stage(PAIRS, True, proj=False)

            hi_late(S_FFN0, 0, KD, 16)
            for k in range(KD):
                act.wait_ge(out_used, KD + k + 1)
                x_hi(k, V_F0)
            hi_late(S_FFN0 + 1, 1, KD, 16)
            for k in range(KD):
                x_square(k, k % 2, KD + k)

            def gate_up(s0, q0, f0, next_tiles):
                hi_late(s0 + 2, 2, KD, 16 * (q0 // 4 + 1))

                def body(i, last):
                    for h in range(2):
                        f = 2 * i + (f0 + h)
                        for e in range(2):
                            b = 2 * h + e + 3
                            tiles = next_tiles if last and b >= 4 else KD
                            hi_late(4 * i + (s0 + b), b % 4, tiles, 64 * 0 + 16 * (i + (q0 // 4 + b // 4 + 1)))
                            if e == 0:
                                act.wait_ge(lin_ready, f + 1)
                                act.activation(g_act[:, 0, :], tmp[:, 0, :], ACT.Silu).then_inc(silu_done, 1)
                                act.wait_ge(h_f, f + 1)
                                dst = h_hi[:, f - f0, :] if isinstance(i, int) else \
                                    h_hi[:, bass.ds(2 * i + h, 1), :].rearrange("p a t -> p (a t)")
                                act.activation(dst, g_act[:, 1, :], ACT.Copy).then_inc(h_h, 1)

                n = GU_SLOTS // 4
                with act.Fori(0, n - 1) as i:
                    body(i, False)
                body(n - 1, True)

            def down(s1, q1, col=None, m0=0):
                def body(i, last):
                    for b in range(3, 7):
                        tiles = HALF if b == 3 or not last else KD
                        if b == 3 or not last or col is not None:
                            hi_late(4 * i + (s1 + b), b % 4, tiles, 16 * (i + (q1 // 4 + b // 4 + 1)))
                        if col is not None and b in (3, 5):
                            n = 2 * i + (b - 3) // 2
                            act.wait_ge(dn_used, n + 1)
                            x_hi(n, col)
                            x_square(n, (b - 3) // 2, n + m0)
                        if last and b == 5:
                            break

                for i in range(DN_SLOTS // 4):
                    body(i, i == DN_SLOTS // 4 - 1)

            gate_up(S_FFN0, 0, 0, HALF)
            down(S_DN0, GU_SLOTS, V_CD, 2 * KD)
            q_cd = GU_SLOTS + DN_SLOTS

            n_cat = 0
            products = [0]

            def pool_tap():
                d = products[0]
                if d == C_TAPS:
                    return
                w = V_CW + C_TAPS - 1 - d
                if d == 0:
                    act.wait_ge(c_ready, 1)
                    act.activation(c_acc[:, 0, :], c_in[:, 0, :], ACT.Identity, scale=vecs[:, w:w + 1],
                                   bias=vecs[:, V_CB:V_CB + 1]).then_inc(prod_ready, 1)
                else:
                    if d > 3:
                        act.wait_ge(prod_added, d - 3)
                    act.activation(prods[:, d % 3, :], c_in[:, 0, :], ACT.Identity, scale=vecs[:, w:w + 1])\
                        .then_inc(prod_ready, 1)
                products[0] += 1

            for q in range(CD_SLOTS + CDO_SLOTS):
                hi_late(S_CD + q + 2, (q + 2) % 4, KD, 16 * ((q_cd + q + 2) // 4 + 1))
                if q < 8 and q % 2:
                    i = q // 2
                    act.wait_ge(cd_used, 2 * i + 2)
                    act.activation(c_sig[:, i % 2, :], c_gate[:, i % 2, :], ACT.Sigmoid).then_inc(cgate_act, 1)
                if 1 <= q < 17:
                    for _ in range(2):
                        pool_tap()
                if q >= 24:
                    for k in (2 * (q - 24), 2 * (q - 24) + 1):
                        act.wait_ge(cd_used, 28 + k + 1)
                        x_hi(k, V_F1)
                        x_square(k, k % 2, 3 * KD + 4 + k)
                if 8 <= q < 20 and (q - 8) % 3 == 2:
                    act.wait_ge(ccat_f, n_cat + 1)
                    act.activation(ccat_hi[:, 4 + n_cat, :], d_out[:, n_cat % 2, :], ACT.Copy).then_inc(ccat_h, 1)
                    n_cat += 1
                if q == 21:
                    for i in range(4):
                        act.wait_ge(xc_ready, i + 1)
                        act.wait_ge(sq_used, 3 * KD + i - 1)
                        act.activation(sq_buf[:, i % 2, :], c_acc[:, i, :], ACT.Square).then_inc(sq_ready, 1)
                if q == 22:
                    for i in range(4):
                        act.wait_ge(cn_ready, i + 1)
                        act.activation(c_in[:, i, :], c_acc[:, i, :], ACT.Silu, scale=vecs[:, V_LG + i:V_LG + i + 1],
                                       bias=vecs[:, V_LB + i:V_LB + i + 1]).then_inc(csilu_done, 1)
                        act.wait_ge(csilu_done, i + 1)
                        act.activation(ccat_hi[:, i, :], c_in[:, i, :], ACT.Copy).then_inc(ccat_h, 1)

            q_f1 = q_cd + CD_SLOTS + CDO_SLOTS
            gate_up(S_FFN1, q_f1, NF, HALF)
            down(S_DN1, q_f1 + GU_SLOTS)

        @block.tensor
        def _(pe):
            def passes(out_, hi, lo, t, m_hi, m_lo, first, last):
                w_hi, w_lo = hi[:, t * P:(t + 1) * P], lo[:, t * P:(t + 1) * P]
                pe.matmul(out_, w_hi, m_hi, start=first, stop=False)
                pe.matmul(out_, w_hi, m_lo, start=False, stop=False)
                return pe.matmul(out_, w_lo, m_hi, start=False, stop=last)

            def project(s, hi_lo, bank, act_hi, act_lo, kts=range(KD), ready=None):
                pe.wait_ge(lo_ready, s + 1)
                for t, k in enumerate(kts):
                    if ready is not None:
                        pe.wait_ge(ready[0], ready[1] + k + 1)
                    last = passes(ps[:, bank, :], *hi_lo, t, act_hi[:, k, :], act_lo[:, k, :], t == 0,
                                  t == len(kts) - 1)
                last.then_inc(slot_done, 1)

            def norm_sums(which, mean_col):
                pe.wait_ge(sq_used, (8, 16, 24, 28, 36)[which - 1])
                for r in range(TB):
                    last = pe.matmul(ps[:, STAT, r:r + 1], sq_acc[:, r * P:(r + 1) * P],
                                     consts[:, mean_col:mean_col + 1], start=True, stop=True)
                last.then_inc(stat_ready, 1)

            def norm_spread(which):
                pe.wait_ge(rstd_tok, which)
                for r in range(TB):
                    last = pe.transpose(ps[:, BC, r * P:(r + 1) * P],
                                        rstd_t[:, r:r + 1].to_broadcast([P, P]), ident)
                last.then_inc(bc_ready, 1)

            def norm(which, mean_col=C_1024):
                norm_sums(which, mean_col)
                norm_spread(which)

            for j in range(A_SLOTS):
                if j >= 5:
                    pe.wait_ge(a_lin, j - 4)
                project(j, hi_lo_ab(j), j % 5, xg_hi, xg_lo, ready=(xg_ready, 0) if j == 0 else None)
                if j == 1:
                    pe.wait_ge(const_loaded, 16)
                    norm(1)

            def score(j, n):
                h, r = divmod(j, TB)
                rows_ = slice(64 * h, 64 * h + 64)
                cls = slice(r * P, (r + 1) * P)
                if j:
                    pe.wait_ge(scores_used, n)
                pe.matmul(scores[:, 0:T], qk_cur[rows_, 0, cls], qk_cur[rows_, 1, :], start=True, stop=True)
                pe.matmul(scores[:, T:T + P], qk_cur[rows_, 2, cls], qk_cur[rows_, 3, cls], start=True, stop=True)
                pe.matmul(scores[:, T + P:KEYS], qk_cur[rows_, 4, cls], qk_cur[rows_, 5, cls], start=True, stop=True)\
                    .then_inc(scores_ready, 1)

            def turn(n):
                pe.wait_ge(probs_ready, n + 1)
                for c in range(KEYS // P):
                    last = pe.transpose(probsT[:, c * P:(c + 1) * P], prob[:, c * P:(c + 1) * P], ident)
                last.then_inc(pt_ready, 1)

            def weigh(j, n):
                h, r = divmod(j, TB)
                pe.wait_ge(pt_out, n + 1)
                blocks = [(0, c) for c in range(TB)] + [(1, r), (2, r)]
                for c, (g, blk) in enumerate(blocks):
                    last = pe.matmul(ps[64 * h:64 * h + 64, OB, r * P:(r + 1) * P],
                                     v_cur[:, g, blk, 64 * h:64 * h + 64], prob_t[:, c * P:(c + 1) * P],
                                     start=(c == 0), stop=(c == len(blocks) - 1))
                last.then_inc(pv_done, 1)

            def misc_done_before(k):
                pe.wait_ge(misc_used, k)

            def turn_v(g, st, k):
                misc_done_before(k)
                if g == 0:
                    pe.wait_ge(qkv_used, 9 * st)
                for r in range(TB):
                    last = pe.transpose(ps[:, MISC, r * P:(r + 1) * P], v_raw[:, g, r * P:(r + 1) * P], ident)
                last.then_inc(misc_ready, 1)

            def head_sums(b, k, st):
                misc_done_before(k)
                pe.wait_ge(qkv_used, 9 * st + 2 * b + 2)
                for t in range(2):
                    for r in range(TB):
                        c = (t * TB + r) * 2
                        last = pe.matmul(ps[:, MISC, c:c + 2], sq_buf[:, t, r * P:(r + 1) * P],
                                         consts[:, C_HM:C_HM + 2], start=True, stop=True)
                last.then_inc(misc_ready, 1)

            def head_spread(b, t, k, st):
                misc_done_before(k)
                pe.wait_ge(rq_ready, 3 * st + b + 1)
                for r in range(TB):
                    c = (t * TB + r) * 2
                    last = pe.transpose(ps[:, MISC, r * P:(r + 1) * P],
                                        wide[:, c * 64:(c + 2) * 64], ident)
                last.then_inc(misc_ready, 1)

            def pair_stage(st, attn, proj=True):
                base = misc_base(st, attn)
                nv = 3 if attn else 0
                for j in range(NB_SLOTS):
                    n = 8 * (st - 1) + j
                    s = S_PAIR + 9 * st + j
                    if attn and j < 8:
                        if j == 0:
                            pe.wait_ge(qk_cur_ready, 6 * st)
                            pe.wait_ge(masks_loaded, 16)
                        score(j, n)
                    if attn and j >= 1:
                        turn(n - 1)
                    if attn and j == 0:
                        turn_v(0, st, base)
                    if attn and j == 1:
                        turn_v(2, st, base + 2)
                    if proj:
                        if j in (2, 4, 6):
                            head_sums(j // 2 - 1, base + nv + 3 * (j // 2 - 1), st)
                        if j in (3, 5, 7):
                            b = (j - 3) // 2
                            head_spread(b, 1, base + nv + 3 * b + 2, st)
                        if j == 8:
                            misc_done_before(base + nv + 9)
                        elif j >= 2:
                            pe.wait_ge(qkv_used, 9 * st + j - 1)
                        elif attn:
                            pe.wait_ge(qkv_used, 9 * st - 3 + j + 1)
                        else:
                            pe.wait_ge(a_lin, 6 + j)
                        project(s, hi_lo_ab(S_PAIR + j), MISC if j == 8 else j % 2, xg_hi, xg_lo)
                    if not proj and j < 8:
                        if j < 2:
                            pe.wait_ge(qkv_used, 9 * st)
                        else:
                            pe.wait_ge(out_used, j - 1)
                        project(s, hi_lo_ab(S_PAIR + j), j % 2, cat_hi, cat_lo, kts=range(KD - 1),
                                ready=(cat_l, 0) if j == 0 else None)
                    if proj and not attn and j == 0:
                        pe.wait_ge(gelu_done, 4)
                        pe.wait_ge(a_lin, A_SLOTS)
                        for c in range(TB):
                            for g in range(4):
                                last = pe.transpose(ps[:, SC + c, g * P:(g + 1) * P],
                                                    vg[:, g, c * P:(c + 1) * P], ident)
                            last.then_inc(vt_ready, 1)
                    if attn and j == 0:
                        turn_v(1, st, base + 1)
                    if proj and j in (2, 4, 6):
                        b = j // 2 - 1
                        head_spread(b, 0, base + nv + 3 * b + 1, st)
                    if proj and not attn and j == 5:
                        pe.wait_ge(ln_ready, 4)
                        pe.wait_ge(sguw_masked, 1)
                        for g in range(4):
                            for c in range(TB):
                                last = pe.matmul(ps[:, SC + g, c * P:(c + 1) * P], vg[:, c, g * P:(g + 1) * P],
                                                 sguw[:, g, :], start=True, stop=True)
                            last.then_inc(mix_ready, 1)
                    if attn and j >= 1:
                        if j == 1:
                            pe.wait_ge(misc_used, base + 3)
                            pe.wait_ge(cat_f, 3 + st)
                        weigh(j - 1, n - 1)

            pair_stage(0, False)
            with pe.Fori(1, PAIRS) as st:
                pair_stage(st, True)
            pair_stage(PAIRS, True, proj=False)
            s = AB_SLOTS - 1
            pe.wait_ge(lo_ready, s + 1)
            pe.wait_ge(cat_l, 8)
            hi, lo = hi_lo_ab(s)
            for n in range(KD):
                pe.wait_ge(out_used, max(KD, 6 + n))
                last = passes(ps[:, n % 3, :], hi, lo, n, cat_hi[:, KD - 1, :], cat_lo[:, KD - 1, :], True, True)
                last.then_inc(out_ready if n < KD - 1 else slot_done, 1)

            def gate_up(s0, q0, f0, which):
                def body(i, first):
                    for b in range(4):
                        if not first:
                            pe.wait_ge(up_used if b % 2 else lin_ready, 2 * i + (f0 + b // 2 - 1))
                        elif b == 0:
                            pe.wait_ge(*((out_used, 2 * KD) if which == 2 else (cd_used, CD_SLOTS + 2 * CDO_SLOTS)))
                        project(4 * i + (s0 + b), hi_lo_late(b, KD), b, xg_hi, xg_lo,
                                ready=(xg_ready, xg_base[which]) if first and b == 0 else None)
                        if first and b == 1:
                            norm(norm_index[which])

                body(0, True)
                with pe.Fori(1, GU_SLOTS // 4) as i:
                    body(i, False)

            xg_base = {2: KD, 3: 2 * KD, 4: 3 * KD}
            norm_index = {2: 2, 3: 3, 4: 5}

            def down(s1, f0, n0):
                def body(i, first):
                    for b in range(4):
                        bank = 4 + b // 2
                        hi, lo = hi_lo_late(b, HALF)
                        s_ = 4 * i + (s1 + b)
                        pe.wait_ge(lo_ready, s_ + 1)
                        if not first and b % 2 == 0:
                            pe.wait_ge(dn_used, 2 * i + (n0 + b // 2 - 1))
                        for t in range(HALF):
                            k = (b % 2) * HALF + t
                            if first and b < 2:
                                pe.wait_ge(h_ready, f0 + k + 1)
                            last = passes(ps[:, bank, :], hi, lo, t, h_hi[:, k, :], h_lo[:, k, :], k == 0,
                                          k == NF - 1)
                        last.then_inc(slot_done, 1)

                body(0, True)
                with pe.Fori(1, DN_SLOTS // 4) as i:
                    body(i, False)

            gate_up(S_FFN0, 0, 0, 2)
            down(S_DN0, 0, 0)

            e = 0
            pe.wait_ge(dn_used, KD)
            for q in range(CD_SLOTS):
                if e >= 6:
                    pe.wait_ge(cd_used, e - 5)
                project(S_CD + q, hi_lo_late(q, KD), e % 6, xg_hi, xg_lo, ready=(xg_ready, 2 * KD) if q == 0 else None)
                e += 1
                if q == 1:
                    norm(3)

            def out_slot(m, half):
                nonlocal e
                q = CD_SLOTS + m
                hi, lo = hi_lo_late(q, KD)
                pe.wait_ge(lo_ready, S_CD + q + 1)
                for n in range(2):
                    pe.wait_ge(cd_used, e - 5)
                    for t in range(4):
                        last = passes(ps[:, e % 6, :], hi, lo, 4 * n + t, ccat_hi[:, 4 * half + t, :],
                                      ccat_lo[:, 4 * half + t, :], t == 0, t == 3)
                    if n == 0:
                        last.then_inc(cdo_ready, 1)
                    e += 1
                last.then_inc(slot_done, 1)

            def channel_mean():
                pe.wait_ge(conv, 3 * C_TAPS)
                pe.wait_ge(prod_added, C_TAPS - 1)
                for i in range(4):
                    last = pe.matmul(ps[:, BC, :], consts[:, C_AVG:C_AVG + P], c_acc[:, i, :], start=(i == 0),
                                     stop=(i == 3))
                last.then_inc(mean_ready, 1)

            pe.wait_ge(ccat_l, 4)
            out_slot(0, 1)
            out_slot(1, 1)
            channel_mean()
            out_slot(2, 1)
            norm_sums(4, C_512)
            out_slot(3, 1)
            norm_spread(4)
            pe.wait_ge(ccat_l, 8)
            for m in range(4, 8):
                out_slot(m, 0)

            gate_up(S_FFN1, 0, NF, 4)
            down(S_DN1, NF, KD)

        @block.vector
        def _(v):
            order = [0, 0]

            def link(ins, fence=True):
                order[1] += 1
                ins.then_inc(dve, 1)
                if fence:
                    v.wait_ge(dve, order[0] + order[1])

            def gate():
                link(v.memset(gate_cell[:], 0.0), fence=False)

            def rsqrt(n):
                m, y, t, h = (z[:, 0:n] for z in (st_m, st_y, st_t, st_h))
                link(v.tensor_scalar(t.bitcast(I32), m.bitcast(I32), 1, None, ALU.logical_shift_right), fence=False)
                link(v.tensor_scalar(h, m, -0.5, None, ALU.mult))
                link(v.tensor_scalar(y.bitcast(I32), t.bitcast(I32), -1.0, MAGIC, ALU.mult, ALU.add))
                for _ in range(3):
                    link(v.tensor_tensor(t, y, y, ALU.mult))
                    link(v.tensor_tensor(t, t, h, ALU.mult))
                    link(v.scalar_tensor_tensor(out=y, in0=t, scalar=1.5, in1=y, op0=ALU.add, op1=ALU.mult))

            def x_lo(k, col, count):
                gain = vecs[:, col + k:col + k + 1]
                v.wait_ge(xh_ready, count)
                v.scalar_tensor_tensor(out=xg_lo[:, k, :], in0=xres[:, k, :], scalar=gain,
                                       in1=xg_hi[:, k, :].bitcast(F32), op0=ALU.mult, op1=ALU.subtract)\
                    .then_inc(xg_ready, 1)

            def norm_finish(which, spread=True):
                v.wait_ge(stat_ready, which)
                link(v.tensor_scalar(st_m[:, 0:TB], ps[:, STAT, 0:TB], EPS, None, ALU.add))
                rsqrt(TB)
                v.tensor_copy(rstd_t[:], st_y[:, 0:TB]).then_inc(rstd_tok, 1)
                if spread:
                    v.wait_ge(bc_ready, which)
                    v.tensor_copy(rstd_b[:], ps[:, BC, :]).then_inc(rstd_ready, 1)
                    v.wait_ge(rstd_ready, rstd_count[which])

            rstd_count = {1: 1, 2: 2, 3: 3, 5: 4}

            def add_square(h, m, restart=False):
                v.wait_ge(sq_ready, m + 1)
                if restart:
                    v.tensor_copy(sq_acc[:], sq_buf[:, h, :]).then_inc(sq_used, 1)
                else:
                    v.wait_ge(sq_used, m)
                    v.tensor_tensor(sq_acc[:], sq_acc[:], sq_buf[:, h, :], ALU.add).then_inc(sq_used, 1)

            def scaled(dst, bank):
                return v.tensor_tensor(dst, ps[:, bank, :], rstd_b[:], ALU.mult)

            v.wait_ge(vecs_loaded, 16)
            for k in range(KD):
                x_lo(k, V_AB, k + 1)
            for k in range(KD):
                add_square(k % 2, k, restart=(k == 0))
            norm_finish(1)
            link(v.tensor_tensor(rstd_t2[:], rstd_t[:], rstd_t[:], ALU.mult))
            for j in range(A_SLOTS):
                v.wait_ge(slot_done, j + 1)
                if j >= 2:
                    v.wait_ge(gelu_done, j - 1)
                scaled(tmp[:, j % 2, :], j % 5).then_inc(a_lin, 1)

            def scores_to_softmax(j, n):
                v.wait_ge(masks_loaded, 16)
                v.wait_ge(scores_ready, n + 1)
                gate()
                v.tensor_tensor_reduce(out=sm[:], in0=scores, in1=masks[:, j % TB, :], scale=-0.125, scalar=BIG,
                                       op0=ALU.add, op1=ALU.min, accum_out=nmax[:, j % 2:j % 2 + 1])\
                    .then_inc(scores_used, 1)

            def normalise(j, n):
                v.wait_ge(exp_done, n + 1)
                link(v.reciprocal(rden[:, j % 2:j % 2 + 1], den[:, j % 2:j % 2 + 1]))
                v.tensor_scalar(prob[:], prob[:], rden[:, j % 2:j % 2 + 1], None, ALU.mult).then_inc(probs_ready, 1)

            def v_out(g, k):
                v.wait_ge(misc_ready, k + 1)
                v.tensor_tensor(v_cur[:, g, :, :], ps[:, MISC, :].rearrange("p (r c) -> p r c", r=TB),
                                rstd_t[:, :].unsqueeze(2).to_broadcast([P, TB, P]), ALU.mult).then_inc(misc_used, 1)

            def head_factors(b, k):
                v.wait_ge(misc_ready, k + 1)
                shape = [P, 2, TB, 2]
                m4 = st_m[:, 0:16].rearrange("p (t r h) -> p t r h", t=2, r=TB)
                for t in range(2):
                    ins = v.tensor_tensor(m4[:, t, :, :],
                                          ps[:, MISC, 8 * t:8 * t + 8].rearrange("p (r h) -> p r h", r=TB),
                                          rstd_t2[:, :].unsqueeze(2).to_broadcast([P, TB, 2]), ALU.mult)
                    link(ins, fence=(t == 1))
                ins = v.tensor_scalar(st_m[:, 0:16], st_m[:, 0:16], EPS, None, ALU.add)
                ins.then_inc(misc_used, 1)
                v.wait_ge(misc_used, k + 1)
                rsqrt(16)
                y4 = st_y[:, 0:16].rearrange("p (t r h) -> p t r h", t=2, r=TB)
                for t in range(2):
                    ins = v.tensor_tensor(wide[:].rearrange("p (t r h d) -> p t r h d", t=2, r=TB, h=2)[:, t],
                                          y4[:, t, :, :].unsqueeze(3).to_broadcast([P, TB, 2, 64]),
                                          rstd_t[:, :].unsqueeze(2).unsqueeze(3).to_broadcast([P, TB, 2, 64]), ALU.mult)
                ins.then_inc(rq_ready, 1)

            def head_scale(b, t, k):
                tile_ = 2 * b + t
                v.wait_ge(misc_ready, k + 1)
                v.scalar_tensor_tensor(out=qk_next[:, tile_, :], in0=qk_next[:, tile_, :],
                                       scalar=vecs[:, V_QK + tile_:V_QK + tile_ + 1], in1=ps[:, MISC, :],
                                       op0=ALU.mult, op1=ALU.mult).then_inc(misc_used, 1)
                v.wait_ge(misc_used, k + 1)

            half_turn = [i + 8 if i < 8 else i - 8 if i < 16 else i for i in range(32)]

            def rotate(b):
                both = qk_next[:, 2 * b:2 * b + 2, :]
                v.wait_ge(dve, order[0] + order[1])
                gate()
                link(v.stream_shuffle(tmp[:], both, half_turn), fence=False)
                link(v.tensor_tensor(both, both, rope[:, 0:1, :].to_broadcast([P, 2, T]), ALU.mult), fence=False)
                v.wait_ge(dve, order[0] + (order[1] - 1))
                link(v.tensor_tensor(tmp[:], tmp[:], rope[:, 1:2, :].to_broadcast([P, 2, T]), ALU.mult))
                link(v.tensor_tensor(both, both, tmp[:], ALU.add))

            def attention_out(st):
                v.wait_ge(pv_done, 8 * st)
                v.tensor_copy(natural(tmp[:, 0, :]), classes(ps[:, OB, :])).then_inc(cat_f, 1)
                v.wait_ge(cat_h, 4 + st)
                dyn = (slice(None), bass.ds(st + 3, 1), slice(None))
                if isinstance(st, int):
                    hi, lo = cat_hi[:, st + 3, :], cat_lo[:, st + 3, :]
                else:
                    hi, lo = (z[dyn].rearrange("p a t -> p (a t)") for z in (cat_hi, cat_lo))
                v.tensor_tensor(lo, tmp[:, 0, :], hi.bitcast(F32), ALU.subtract).then_inc(cat_l, 1)
                v.wait_ge(cat_l, 4 + st)

            def pair_stage(st, attn, proj=True):
                base = misc_base(st, attn)
                nv = 3 if attn else 0
                for j in range(NB_SLOTS):
                    n = 8 * (st - 1) + j
                    if attn and j < 8:
                        scores_to_softmax(j, n)
                    if attn and j == 0:
                        v_out(0, base)
                    if attn and j == 1:
                        v_out(2, base + 2)
                    if proj and not attn and j == 0:
                        gmlp_norm()
                    if proj and j in (2, 4, 6):
                        head_factors(j // 2 - 1, base + nv + 3 * (j // 2 - 1))
                    if proj and j in (3, 5, 7):
                        b = (j - 3) // 2
                        head_scale(b, 1, base + nv + 3 * b + 2)
                    if attn and j < 8:
                        normalise(j, n)
                    if proj and j in (3, 5, 7):
                        rotate((j - 3) // 2)
                    if attn and j == 0:
                        v_out(1, base + 1)
                    if proj and j in (2, 4, 6):
                        b = j // 2 - 1
                        head_scale(b, 0, base + nv + 3 * b + 1)
                    if proj and not attn and j == 6:
                        gmlp_gate()
                    if not proj and j < 8:
                        v.wait_ge(slot_done, S_PAIR + 9 * st + j + 1)
                        if j == 0:
                            v.wait_ge(xnat_loaded, 16)
                        v.tensor_tensor(xres[:, j, :], xres[:, j, :], ps[:, j % 2, :], ALU.add).then_inc(out_used, 1)
                if proj:
                    for b in range(3):
                        v.tensor_copy(qk_cur[:, 2 * b:2 * b + 2, :], qk_next[:, 2 * b:2 * b + 2, :])\
                            .then_inc(qk_cur_ready, 2)
                if attn:
                    attention_out(st)

            def gmlp_norm():
                v.wait_ge(vt_ready, 4)
                v.wait_ge(gelu_done, A_SLOTS)
                v.wait_ge(a_loaded, 32)
                for c in range(TB):
                    link(v.bn_stats(bn[:, c, :], ps[:, SC + c, :]), fence=(c == TB - 1))
                for c in range(TB):
                    link(v.bn_aggr(mv[:, c, :], bn[:, c, :]), fence=(c == TB - 1))
                link(v.tensor_scalar(st_m[:, 0:TB], mv[:, :, 1], EPS, None, ALU.add))
                rsqrt(TB)
                for c in range(TB):
                    link(v.tensor_scalar(vg[:, c, :], ps[:, SC + c, :], mv[:, c, 0:1], st_y[:, c:c + 1], ALU.subtract,
                                         ALU.mult), fence=(c == TB - 1))
                for c in range(TB):
                    link(v.tensor_tensor(vg[:, c, :], vg[:, c, :], rows[:, 0, :], ALU.mult), fence=(c == TB - 1))
                for c in range(TB):
                    v.tensor_tensor(vg[:, c, :], vg[:, c, :], rows[:, 1, :], ALU.add).then_inc(ln_ready, 1)

            def gmlp_gate():
                for g in range(4):
                    v.wait_ge(mix_ready, g + 1)
                    if g >= 2:
                        v.wait_ge(cat_l, g - 1)
                    dst = tmp[:, g % 2, :]
                    bias = rows[:, 2, g * P:(g + 1) * P].unsqueeze(1).to_broadcast([P, TB, P])
                    link(v.tensor_tensor(dst.rearrange("p (c t) -> p c t", c=TB),
                                         ps[:, SC + g, :].rearrange("p (c t) -> p c t", c=TB), bias, ALU.add))
                    v.tensor_tensor(dst, dst, u[:, g, :], ALU.mult).then_inc(cat_f, 1)
                    if g >= 1:
                        gmlp_lo(g - 1)
                gmlp_lo(3)

            def gmlp_lo(g):
                v.wait_ge(cat_h, g + 1)
                v.tensor_tensor(cat_lo[:, g, :], tmp[:, g % 2, :], cat_hi[:, g, :].bitcast(F32), ALU.subtract)\
                    .then_inc(cat_l, 1)

            v.wait_ge(rope_loaded, 16)
            pair_stage(0, False)
            start = order[1]
            per = LOOP_STEPS
            with v.Fori(1, PAIRS) as st:
                order[0], order[1] = (st - 1) * per + start, 0
                pair_stage(st, True)
                assert order[1] == per, order[1]
            order[0], order[1] = 0, start + 3 * per
            pair_stage(PAIRS, True, proj=False)
            for n in range(KD):
                v.wait_ge(*((out_ready, n + 1) if n < KD - 1 else (slot_done, AB_SLOTS)))
                v.tensor_tensor(xres[:, n, :], xres[:, n, :], ps[:, n % 3, :], ALU.add).then_inc(out_used, 1)
                if n >= 1:
                    x_lo(n - 1, V_F0, KD + n)
            x_lo(KD - 1, V_F0, 2 * KD)
            for k in range(KD):
                add_square(k % 2, KD + k, restart=(k == 0))

            def gate_up(s0, f0):
                with v.Fori(0, NF // 2) as i:
                    for h in range(2):
                        f = 2 * i + (f0 + h)
                        v.wait_ge(slot_done, 4 * i + (s0 + 2 * h + 1))
                        scaled(tmp[:, 0, :], 2 * h).then_inc(lin_ready, 1)
                        v.wait_ge(slot_done, 4 * i + (s0 + 2 * h + 2))
                        scaled(tmp[:, 1, :], 2 * h + 1).then_inc(up_used, 1)
                        v.wait_ge(up_used, f + 1)
                        v.wait_ge(silu_done, f + 1)
                        v.tensor_tensor(g_act[:, 1, :], g_act[:, 0, :], tmp[:, 1, :], ALU.mult).then_inc(h_f, 1)
                        v.wait_ge(h_h, f + 1)
                        hi, lo = (z[:, bass.ds(2 * i + h, 1), :].rearrange("p a t -> p (a t)") for z in (h_hi, h_lo))
                        v.tensor_tensor(lo, g_act[:, 1, :], hi.bitcast(F32), ALU.subtract).then_inc(h_ready, 1)

            def down(s1, n0, col=None, m0=0):
                for n in range(KD):
                    v.wait_ge(slot_done, s1 + 2 * n + 2)
                    v.tensor_tensor(xres[:, n, :], xres[:, n, :], ps[:, 4 + n % 2, :], ALU.add).then_inc(dn_used, 1)
                    if col is not None:
                        x_lo(n, col, m0 + n + 1)
                        add_square(n % 2, m0 + n, restart=(n == 0))

            norm_finish(2)
            gate_up(S_FFN0, 0)
            down(S_DN0, 0, V_CD, 2 * KD)
            norm_finish(3)

            steps = {i: [] for i in range(1, 4)}

            def conv_steps(count, ready):
                while count:
                    open_ = [i for i in range(1, ready) if len(steps[i]) < C_TAPS]
                    if not open_:
                        return
                    i = min(open_, key=lambda t: steps[t][-1] if steps[t] else -1)
                    d = len(steps[i])
                    w = V_CW + i * C_TAPS + C_TAPS - 1 - d
                    if d == 0:
                        ins = v.tensor_scalar(c_acc[:, i, :], c_in[:, i, :], vecs[:, w:w + 1],
                                              vecs[:, V_CB + i:V_CB + i + 1], ALU.mult, ALU.add)
                    else:
                        v.wait_ge(conv, steps[i][-1])
                        ins = v.scalar_tensor_tensor(out=c_acc[:, i, d:T], in0=c_in[:, i, 0:T - d],
                                                     scalar=vecs[:, w:w + 1], in1=c_acc[:, i, d:T], op0=ALU.mult,
                                                     op1=ALU.add)
                    ins.then_inc(conv, 1)
                    steps[i].append(sum(map(len, steps.values())) + 1)
                    count -= 1

            for i in range(4):
                v.wait_ge(slot_done, S_CD + 2 * i + 1)
                scaled(tmp[:, i % 2, :], (2 * i) % 6).then_inc(cd_used, 1)
                v.wait_ge(slot_done, S_CD + 2 * i + 2)
                if i >= 2:
                    v.wait_ge(cgate_act, i - 1)
                scaled(c_gate[:, i % 2, :], (2 * i + 1) % 6).then_inc(cd_used, 1)
                v.wait_ge(cgate_act, i + 1)
                v.tensor_tensor(c_in[:, i, :], tmp[:, i % 2, :], c_sig[:, i % 2, :], ALU.mult).then_inc(c_ready, 1)
                v.wait_ge(c_ready, i + 1)
                conv_steps(CONV_EARLY if i >= 1 else 0, i + 1)
            for i in range(4):
                b = 8 + 3 * i
                v.wait_ge(slot_done, S_CD + b + 1)
                scaled(tmp[:, 0, :], b % 6).then_inc(cd_used, 1)
                conv_steps(CONV_STEP, 4)
                v.wait_ge(slot_done, S_CD + b + 2)
                scaled(tmp[:, 1, :], (b + 1) % 6).then_inc(cd_used, 1)
                v.wait_ge(cd_used, b + 2)
                y, z = d_y[:, i % 2, :], d_z[:, i % 2, :]
                link(v.tensor_tensor(y, tmp[:, 0, :], tmp[:, 1, :], ALU.mult))
                w = V_DW + i * D_TAPS
                link(v.tensor_scalar(z, y, vecs[:, w + 2:w + 3], None, ALU.mult))
                for d in (1, 2):
                    link(v.scalar_tensor_tensor(out=z[:, d:T], in0=y[:, 0:T - d], scalar=vecs[:, w + 2 - d:w + 3 - d],
                                                in1=z[:, d:T], op0=ALU.mult, op1=ALU.add))
                conv_steps(CONV_STEP, 4)
                v.wait_ge(slot_done, S_CD + b + 3)
                scaled(tmp[:, 0, :], (b + 2) % 6).then_inc(cd_used, 1)
                v.wait_ge(cd_used, b + 3)
                v.tensor_tensor(d_out[:, i % 2, :], z, tmp[:, 0, :], ALU.mult).then_inc(ccat_f, 1)
                conv_steps(CONV_STEP, 4)
                v.wait_ge(ccat_h, i + 1)
                v.tensor_tensor(ccat_lo[:, 4 + i, :], d_out[:, i % 2, :], ccat_hi[:, 4 + i, :].bitcast(F32),
                                ALU.subtract).then_inc(ccat_l, 1)
            e = CD_SLOTS

            def add_out(m):
                nonlocal e
                for n in range(2):
                    if n == 0:
                        v.wait_ge(cdo_ready, m + 1)
                    else:
                        v.wait_ge(slot_done, S_CD + CD_SLOTS + m + 1)
                    t = 2 * (m % 4) + n
                    v.tensor_tensor(xres[:, t, :], xres[:, t, :], ps[:, e % 6, :], ALU.add).then_inc(cd_used, 1)
                    e += 1

            conv_steps(3 * C_TAPS, 4)
            add_out(0)
            add_out(1)
            v.wait_ge(mean_ready, 1)
            for i in range(4):
                v.tensor_tensor(c_acc[:, i, :], c_acc[:, i, :], ps[:, BC, :], ALU.subtract).then_inc(xc_ready, 1)
            for i in range(4):
                add_square(i % 2, 3 * KD + i, restart=(i == 0))
            add_out(2)
            norm_finish(4, spread=False)
            add_out(3)
            v.wait_ge(bc_ready, 4)
            for i in range(4):
                v.tensor_tensor(c_acc[:, i, :], c_acc[:, i, :], ps[:, BC, :], ALU.mult).then_inc(cn_ready, 1)
            for i in range(4):
                v.wait_ge(ccat_h, 4 + i + 1)
                v.tensor_tensor(ccat_lo[:, i, :], c_in[:, i, :], ccat_hi[:, i, :].bitcast(F32), ALU.subtract)\
                    .then_inc(ccat_l, 1)
            for m in range(4, 8):
                v.wait_ge(cd_used, e - 6)
                add_out(m)
                for k in (2 * m - 8, 2 * m - 7):
                    x_lo(k, V_F1, 3 * KD + k + 1)
                for k in (2 * m - 8, 2 * m - 7):
                    add_square(k % 2, 3 * KD + 4 + k, restart=(k == 0))
            norm_finish(5)
            gate_up(S_FFN1, NF)
            down(S_DN1, KD)


LOOP_STEPS = 8 * 2 + 3 * (2 + 12 + 5)
CONV_EARLY = 10
CONV_STEP = 6


def misc_base(st, attn):
    return 9 + 12 * (st - 1) if attn else 0


def misc_ssq(st, b, attn):
    return misc_base(st, attn) + (3 if attn else 0) + 3 * b + 1



def _tiles(w, cols, rows):
    import numpy as np
    return np.concatenate([w[k * 128:(k + 1) * 128, c:c + 128] for k, c in zip(rows, cols)], axis=1)


def kernel(**inputs):
    import numpy as np
    import concourse.bacc as _bacc
    from concourse import mybir as _mybir
    from concourse.bass_utils import run_bass_kernel_spmd as _run

    a = {k: np.asarray(v) for k, v in inputs.items()}
    f = np.float32
    k8 = list(range(KD))

    def slot(w, c, ks=k8):
        return _tiles(w, [c] * len(ks), ks)

    w_in, w_out = a["ab_w_in"][0], a["ab_w_out"][0]
    A2 = 1024
    slots = [slot(w_in, 512 + 128 * g) for g in range(4)] + [slot(w_in, 128 * g) for g in range(4)]
    for p in range(PAIRS):
        for g in range(3):
            for which in range(2):
                slots.append(slot(w_in, A2 + which * 1536 + g * 512 + 128 * p))
        for g in range(3):
            slots.append(slot(w_in, A2 + 2 * 1536 + g * 512 + 128 * p))
    for n in range(8):
        slots.append(np.concatenate([slot(w_out, 128 * n, k8[:7]), np.zeros((128, 128), f)], axis=1))
    slots.append(_tiles(w_out, [128 * n for n in range(8)], [7] * 8))

    def gate_up(layer):
        r = []
        for t in range(NF):
            r += [slot(a["ffn_w_gate"][layer], 128 * t), slot(a["ffn_w_up"][layer], 128 * t)]
        return r

    def down(layer):
        w = a["ffn_w_down"][layer]
        return np.stack([slot(w, 128 * n, list(range(HALF * h, HALF * h + HALF))) for n in range(8) for h in range(2)])

    w_ab = np.stack(slots + gate_up(0))
    ci, co = a["cd_w_in"][0], a["cd_w_out"][0]
    cs = []
    for i in range(4):
        cs += [slot(ci, 128 * i), slot(ci, 512 + 128 * i)]
    for i in range(4):
        cs += [slot(ci, 1536 + 128 * i), slot(ci, 2048 + 128 * i), slot(ci, 1024 + 128 * i)]
    for ks in ([4, 5, 6, 7], [0, 1, 2, 3]):
        for m in range(4):
            cs.append(_tiles(co, [256 * m] * 4 + [256 * m + 128] * 4, ks + ks))
    w_cd = np.stack(cs + gate_up(1))

    x = a["x"][0].T.reshape(KD, 128, T).transpose(1, 0, 2)
    x_nat = np.ascontiguousarray(x)
    x_cls = np.ascontiguousarray(x.reshape(128, KD, 128, 4).transpose(0, 1, 3, 2).reshape(128, KD, T))

    def cols(vec):
        return vec.reshape(-1, 128).T

    qk = []
    for g in range(3):
        for n in ("q_norm_g", "k_norm_g"):
            qk.append(np.concatenate([a[n][0, g], a[n][0, g]])[:, None])

    def taps(w):
        return w.T.reshape(4, 128, w.shape[0]).transpose(1, 0, 2).reshape(128, -1)

    vecs = np.concatenate(qk + [cols(a["ab_norm_g"][0]), cols(a["ffn_norm_g"][0]), cols(a["cd_norm_g"][0]),
                                cols(a["ffn_norm_g"][1]), taps(a["conv_c_w"][0]), cols(a["conv_c_b"][0]),
                                cols(a["c_ln_g"][0]), cols(a["c_ln_b"][0]), taps(a["conv_d_w"][0])], axis=1)
    rows = np.stack([np.broadcast_to(r, (128, 512)) for r in
                     (a["sgu_norm_g"][0], a["sgu_norm_b"][0], a["sgu_bias"][0].reshape(-1))], axis=1)
    sguw = a["sgu_w"][0].transpose(2, 0, 1)

    consts = np.zeros((128, C_N), f)
    consts[:, C_ID:C_ID + 128] = np.eye(128, dtype=f)
    consts[0:64, C_HM] = 1 / 64
    consts[64:128, C_HM + 1] = 1 / 64
    consts[:, C_1024] = 1 / 1024
    consts[:, C_512] = 1 / 512
    consts[:, C_AVG:] = 1 / 512
    i = np.arange(128)
    masks = np.zeros((128, 4, KEYS), f)
    for r in range(4):
        tq = 4 * i + r
        for c in range(4):
            dist = tq[:, None] - (4 * i + c)[None, :]
            masks[:, r, 128 * c:128 * c + 128] = np.where((dist >= 0) & (dist <= 128), 0, -1e30)
        causal = i[:, None] >= i[None, :]
        masks[:, r, 512:640] = np.where(causal, 0, -1e30)
        masks[:, r, 640:768] = np.where(causal & ((i[:, None] - i[None, :]) % 4 == 0), 0, -1e30)
    inv = f(500000.0) ** (-np.arange(8, dtype=f) * f(2.0) / f(16))
    pos = (4 * i[None, :] + np.arange(4)[:, None]).reshape(-1).astype(f)
    ang = (pos[None, :] * inv.astype(f)[:, None]).astype(f)
    rope = np.zeros((128, 2, T), f)
    rope[:, 0, :] = 1
    for h in (0, 64):
        rope[h:h + 8, 0], rope[h + 8:h + 16, 0] = np.cos(ang), np.cos(ang)
        rope[h:h + 8, 1], rope[h + 8:h + 16, 1] = -np.sin(ang), np.sin(ang)

    arrays = {"x_cls": x_cls, "x_nat": x_nat, "w_ab": w_ab, "w_dn0": down(0), "w_cd": w_cd, "w_dn1": down(1),
              "vecs_d": vecs, "consts_d": consts, "rows_d": rows, "sguw_d": sguw, "masks_d": masks, "rope_d": rope}
    nc = _bacc.Bacc("TRN2", target_bir_lowering=False, num_devices=1)
    args = []
    for name in arrays:
        arrays[name] = np.ascontiguousarray(arrays[name])
        args.append(nc.dram_tensor(name, arrays[name].shape, _mybir.dt.float32, kind="ExternalInput").ap())
    out = nc.dram_tensor("out", [KD, 128, T], _mybir.dt.float32, kind="ExternalOutput").ap()
    build(nc, *args, out)
    r = _run(nc, [arrays], core_ids=[0])
    got = np.asarray(r.results[0]["out"])
    return np.ascontiguousarray(got.reshape(D, T).T).reshape(1, T, D)
```

```python
from contextlib import ExitStack

import concourse.bass as bass
from concourse import mybir

F32 = mybir.dt.float32
F32R = mybir.dt.float32r
I32 = mybir.dt.int32
ALU = mybir.AluOpType
ACT = mybir.ActivationFunctionType

P = 128
HEAD = 64
T = 512
D = 1024
KD = D // P
FF = 2816
NF = FF // P
TB = T // P
HALF = NF // 2
PAIRS = 4
NB_SLOTS = 9
A_SLOTS = 8
AB_SLOTS = A_SLOTS + NB_SLOTS * PAIRS + NB_SLOTS
GU_SLOTS = 2 * NF
DN_SLOTS = 2 * KD
CD_SLOTS = 20
CDO_SLOTS = 8
C_TAPS = 31
D_TAPS = 3
PRODS = 8
PIECES = 4
KEYS = T + 2 * P
EPS = 1e-6
MAGIC = 1597463007.0
BIG = 3.0e38

S_PAIR = A_SLOTS
S_FFN0 = AB_SLOTS
S_DN0 = S_FFN0 + GU_SLOTS
S_CD = S_DN0 + DN_SLOTS
S_FFN1 = S_CD + CD_SLOTS + CDO_SLOTS
S_DN1 = S_FFN1 + GU_SLOTS

V_QK = 0
V_AB, V_F0, V_CD, V_F1 = 6, 14, 22, 30
V_CW = 38
V_CB = V_CW + 4 * C_TAPS
V_LG = V_CB + 4
V_LB = V_LG + 4
V_DW = V_LB + 4
V_SG = V_DW + 4 * D_TAPS
V_SB = V_SG + 4
V_N = V_SB + 4
C_ID = 0
C_HM = 128
C_1024 = 130
C_512 = 131
C_AVG = 132
C_ONES = C_AVG + 128
C_N = C_ONES + 128

MISC = 2
SC = 3
PT = 5
WSUM = 5
OB = 7
STAT, BC = 7, 6


def build(nc, x_cls, x_nat, w_ab, w_dn0, w_cd, w_dn1, vecs_d, consts_d, sgu_bias_d, sguw_d, masks_d, rope_d, out):
    with ExitStack() as ctx:
        def alloc(c, name, shape, dt=F32):
            return c.enter_context(nc.sbuf_tensor(name, shape, dt))

        def sem(name):
            return ctx.enter_context(nc.semaphore(name))

        xres = alloc(ctx, "xres", [P, KD, T])
        xg_hi = alloc(ctx, "xg_hi", [P, KD, T], F32R)
        xg_lo = alloc(ctx, "xg_lo", [P, KD, T], F32R)
        raw = alloc(ctx, "raw", [P, 4 * HALF * P])
        split = alloc(ctx, "split", [P, 48 * P], F32R)
        with ExitStack() as norms:
            norm_rows = alloc(norms, "norm_rows", [P, 2, T])
            rstd_b, sq_acc = norm_rows[:, 0, :], norm_rows[:, 1, :]
        qk_lo = alloc(ctx, "qk_lo", [P, 2, T], F32R)
        sq_buf = alloc(ctx, "sq_buf", [P, 2, T])
        tmp = alloc(ctx, "tmp", [P, 2, T])
        vecs = alloc(ctx, "vecs", [P, V_N])
        consts = alloc(ctx, "consts", [P, C_N])
        rstd_t = alloc(ctx, "rstd_t", [P, TB])
        rstd_t2 = alloc(ctx, "rstd_t2", [P, TB])
        st_m = alloc(ctx, "st_m", [P, 16])
        st_y = alloc(ctx, "st_y", [P, 16])
        st_t = alloc(ctx, "st_t", [P, 16])
        st_h = alloc(ctx, "st_h", [P, 16])
        nmax = alloc(ctx, "nmax", [P, 2])
        den = alloc(ctx, "den", [P, 2])
        rden = alloc(ctx, "rden", [P, 2])
        cell = alloc(ctx, "cell", [P, 1])
        gate_cell = alloc(ctx, "gate_cell", [P, 1])
        ident = consts[:, C_ID:C_ID + P]

        with ExitStack() as ab:
            cat_hi = alloc(ab, "cat_hi", [P, KD, T], F32R)
            cat_lo = alloc(ab, "cat_lo", [P, KD, T], F32R)
            rope = alloc(ab, "rope", [P, 2, T])
            qk_next = alloc(ab, "qk_next", [P, 6, T])
            qk_hi = alloc(ab, "qk_hi", [P, 2, T], F32R)
            qk_cur = alloc(ab, "qk_cur", [P, 4, T])
            v_raw = alloc(ab, "v_raw", [P, 3, T])
            wide = alloc(ab, "wide", [P, 2 * T])
            with ExitStack() as a:
                vg = alloc(a, "vg", [P, 4, T])
                gate_bias = alloc(a, "gate_bias", [P, 4, P])
                u = alloc(a, "u", [P, 4, T])
                sguw = alloc(a, "sguw", [P, 4, P])
                sgu_bias = alloc(a, "sgu_bias", [P, 4, P])
                ln_scale = alloc(a, "ln_scale", [P, TB])
                ln_shift = alloc(a, "ln_shift", [P, TB])
                bn = alloc(a, "bn", [P, TB, 6])
                mv = alloc(a, "mv", [P, TB, 2])
            with ExitStack() as b:
                masks_23 = alloc(b, "masks_23", [P, 2, KEYS])
                prob_t = alloc(b, "prob_t", [P, KEYS])
                prob = alloc(b, "prob", [P, KEYS])
                sm = alloc(b, "sm", [P, KEYS])
                v_cur = alloc(b, "v_cur", [P, 3, TB, P])
                masks_01 = alloc(b, "masks_01", [P, 2, KEYS])
                masks = [masks_01[:, 0, :], masks_01[:, 1, :], masks_23[:, 0, :], masks_23[:, 1, :]]
        with ExitStack() as ffn:
            h_hi = alloc(ffn, "h_hi", [P, NF, T], F32R)
            h_lo = alloc(ffn, "h_lo", [P, NF, T], F32R)
            g_act = alloc(ffn, "g_act", [P, 2, T])
        with ExitStack() as cd:
            ccat_hi = alloc(cd, "ccat_hi", [P, KD, T], F32R)
            ccat_lo = alloc(cd, "ccat_lo", [P, KD, T], F32R)
            c_in = alloc(cd, "c_in", [P, 4, T])
            c_acc = alloc(cd, "c_acc", [P, 4, T])
            c_gate = alloc(cd, "c_gate", [P, 2, T])
            c_sig = alloc(cd, "c_sig", [P, 2, T])
            d_y = alloc(cd, "d_y", [P, 2, T])
            d_z = alloc(cd, "d_z", [P, 2, T])
            rstd_sq = alloc(cd, "rstd_sq", [P, T])
            d_out = alloc(cd, "d_out", [P, 2, T])
            prods = alloc(cd, "prods", [P, PRODS, T])

        ps = ctx.enter_context(nc.psum_tensor("ps", [P, 8, T], F32))
        scores = ps[:, SC:SC + 2, :].rearrange("p b t -> p (b t)")[:, 0:KEYS]
        probsT = ps[:, PT:PT + 2, :].rearrange("p b t -> p (b t)")[:, 0:KEYS]

        x_loaded = [sem(f"x_loaded_{k}") for k in range(KD)]
        vecs_loaded, xnat_loaded, const_loaded, a_loaded, rope_loaded = (
            sem(n) for n in ("vecs_loaded", "xnat_loaded", "const_loaded", "a_loaded", "rope_loaded"))
        masks_loaded = [sem(f"masks_loaded_{r}") for r in range(TB)]
        raw3 = [sem(f"raw3_{i}") for i in range(3)]
        raw4 = [sem(f"raw4_{i}") for i in range(4)]
        first_loaded = [sem(f"first_loaded_{c}") for c in range(PIECES - 1)]
        first_hi, first_lo = sem("first_hi"), sem("first_lo")
        hi_ready, lo_ready, slot_done = sem("hi_ready"), sem("lo_ready"), sem("slot_done")
        dve = sem("dve")
        xh_ready, xg_ready, sq_ready, sq_used = sem("xh_ready"), sem("xg_ready"), sem("sq_ready"), sem("sq_used")
        stat_ready, rstd_tok, bc_ready, rstd_ready = (
            sem(n) for n in ("stat_ready", "rstd_tok", "bc_ready", "rstd_ready"))
        a_lin, gelu_done, sguw_masked, vt_ready, ln_ready, mix_ready, cat_f, cat_h, cat_l = (
            sem(n) for n in ("a_lin", "gelu_done", "sguw_masked", "vt_ready", "ln_ready", "mix_ready",
                             "cat_f", "cat_h", "cat_l"))
        qkv_used, qk_cur_ready = sem("qkv_used"), sem("qk_cur_ready")
        scores_ready, scores_used, exp_done, probs_ready, pt_ready, pt_out, pv_done = (
            sem(n) for n in ("scores_ready", "scores_used", "exp_done", "probs_ready", "pt_ready", "pt_out",
                             "pv_done"))
        misc_ready, misc_used, rq_ready = sem("misc_ready"), sem("misc_used"), sem("rq_ready")
        out_ready, out_used = sem("out_ready"), sem("out_used")
        up_used, lin_ready, silu_done, h_f, h_h, h_ready, dn_used = (
            sem(n) for n in ("up_used", "lin_ready", "silu_done", "h_f", "h_h", "h_ready", "dn_used"))
        cd_used, cgate_act, ccat_h, ccat_l, mean_ready, xc_ready = (
            sem(n) for n in ("cd_used", "cgate_act", "ccat_h", "ccat_l", "mean_ready", "xc_ready"))
        dz_ready = sem("dz_ready")
        gate_ready = sem("gate_ready")
        cell_ready = sem("cell_ready")
        q0_ready, qk_hi_ready = sem("q0_ready"), sem("qk_hi_ready")
        qk_lo_ready = sem("qk_lo_ready")
        ln_factors, wsum_ready, sgu_bias_ready = sem("ln_factors"), sem("wsum_ready"), sem("sgu_bias_ready")
        tap0_done = sem("tap0_done")
        conv = [sem(f"conv_{i}") for i in range(4)]
        c_ready, prod_ready, prod_added = sem("c_ready"), sem("prod_ready"), sem("prod_added")
        cn_ready, csilu_done, cdo_ready, stored = (
            sem(n) for n in ("cn_ready", "csilu_done", "cdo_ready", "stored"))

        def raw_ab(s):
            return raw[:, (s % 3) * KD * P:(s % 3 + 1) * KD * P]

        def raw_late(q, tiles):
            return raw[:, (q % 4) * HALF * P:((q % 4) * HALF + tiles) * P]

        def hi_lo_ab(s):
            o = (s % 3) * 16 * P
            return split[:, o:o + KD * P], split[:, o + KD * P:o + 2 * KD * P]

        def hi_lo_late(q, tiles, middle=False):
            if middle:
                return hi_lo_ab(AB_SLOTS - 1)
            o = (q + 1) % 2 * (32 if tiles == KD else 22) * P
            return split[:, o:o + tiles * P], split[:, o + tiles * P:o + 2 * tiles * P]

        def piece(ap, c):
            return ap[:, c * KD * P // PIECES:(c + 1) * KD * P // PIECES]

        def natural(ap):
            return ap.rearrange("p (i r) -> p r i", r=TB)

        def classes(ap):
            return ap.rearrange("p (r i) -> p r i", r=TB)

        block = ctx.enter_context(nc.Block())

        @block.sync
        def _(sp):
            def load(dst, src, s_):
                sp.dma_start(dst, src).then_inc(s_, 16)

            def slot(dram, index, dst, s_):
                load(dst, dram[index, :, :] if isinstance(index, int) else
                     dram[bass.ds(index, 1), :, :].rearrange("a p n -> p (a n)"), s_)

            load(vecs[:], vecs_d, vecs_loaded)
            for k in range(KD):
                if k < PIECES:
                    load(piece(raw_ab(0), k), piece(w_ab[0, :, :], k), first_loaded[k] if k < PIECES - 1 else raw3[0])
                load(xres[:, k, :], x_cls[:, k, :], x_loaded[k])
                if k in (3, 7):
                    s = k // 4 + 1
                    slot(w_ab, s, raw_ab(s), raw3[s])
            load(consts[:], consts_d, const_loaded)
            load(sguw[:], sguw_d, a_loaded)
            load(sgu_bias[:], sgu_bias_d, a_loaded)
            load(rope[:], rope_d, rope_loaded)
            def ring_of_three(i):
                for b in range(3):
                    sp.wait_ge(lo_ready, 3 * i + (b - 2))
                    slot(w_ab, 3 * i + b, raw_ab(b), raw3[b])

            with sp.Fori(1, 5) as i:
                ring_of_three(i)
            sp.wait_ge(mix_ready, 4)
            for r in (0, 1):
                load(masks[r], masks_d[:, r, :], masks_loaded[r])
            ring_of_three(5)
            ring_of_three(6)
            sp.wait_ge(cat_l, 4)
            for r in (2, 3):
                load(masks[r], masks_d[:, r, :], masks_loaded[r])
            sp.wait_ge(xg_ready, KD)
            sp.wait_ge(sq_used, KD)
            load(xres[:], x_nat, xnat_loaded)
            with sp.Fori(7, 17) as i:
                ring_of_three(i)
            for s in (51, 52):
                sp.wait_ge(lo_ready, s - 2)
                slot(w_ab, s, raw_ab(s), raw3[s % 3])

            def phase(dram, start, n, tiles, at, skip=0):
                with sp.Fori(skip, n // 4) as i:
                    for b in range(4):
                        sp.wait_ge(lo_ready, 4 * i + (start + b - 3))
                        slot(dram, 4 * i + (at + b), raw_late(b, tiles), raw4[b])

            sp.wait_ge(lo_ready, AB_SLOTS)
            for b in range(4):
                slot(w_ab, AB_SLOTS + b, raw_late(b, KD), raw4[b])
            phase(w_ab, S_FFN0, GU_SLOTS, KD, AB_SLOTS, skip=1)
            phase(w_dn0, S_DN0, DN_SLOTS, HALF, 0)
            phase(w_cd, S_CD, CD_SLOTS + CDO_SLOTS + GU_SLOTS, KD, 0)
            phase(w_dn1, S_DN1, DN_SLOTS, HALF, 0)
            with sp.Fori(0, KD) as n:
                sp.wait_ge(dn_used, n + (KD + 1))
                sp.dma_start(out[bass.ds(n, 1), :, :].rearrange("a p t -> p (a t)"),
                             xres[:, bass.ds(n, 1), :].rearrange("p a t -> p (a t)")).then_inc(stored, 16)
            sp.wait_ge(stored, 16 * KD)

        @block.gpsimd
        def _(pool):
            def lo_part(s, src, hi_lo):
                hi, lo = hi_lo
                pool.wait_ge(hi_ready, s + 1)
                pool.tensor_tensor(lo, src, hi.bitcast(F32), ALU.subtract).then_inc(lo_ready, 1)

            pool.memset(cell[:], 0.0).then_inc(cell_ready, 1)
            for c in range(PIECES):
                hi, lo = (piece(z, c) for z in hi_lo_ab(0))
                pool.wait_ge(*((first_hi, c + 1) if c < PIECES - 1 else (hi_ready, 1)))
                pool.tensor_tensor(lo, piece(raw_ab(0), c), hi.bitcast(F32), ALU.subtract)\
                    .then_inc(first_lo if c < PIECES - 1 else lo_ready, 1)
            for s in (1, 2):
                lo_part(s, raw_ab(s), hi_lo_ab(s))
            pool.wait_ge(a_loaded, 32)
            pool.affine_select(out=sguw[:], in_=sguw[:], compare_op=ALU.is_ge, fill=0.0, base=0,
                               pattern=[[0, 4], [1, P]], channel_multiplier=-1).then_inc(sguw_masked, 1)
            with pool.Fori(1, 5) as i:
                for b in range(3):
                    lo_part(3 * i + b, raw_ab(b), hi_lo_ab(b))
            for s in range(15, 21):
                lo_part(s, raw_ab(s), hi_lo_ab(s))
                if s == 15:
                    pool.wait_ge(qk_hi_ready, 1)
                    pool.tensor_tensor(qk_lo[:], qk_next[:, 0:2, :], qk_hi[:].bitcast(F32), ALU.subtract)\
                        .then_inc(qk_lo_ready, 1)
                for g in GATED_AT.get(s - S_PAIR - 3, ()):
                    pool.wait_ge(gate_ready, g + 1)
                    pool.tensor_tensor(vg[:, g, :], vg[:, g, :], u[:, g, :], ALU.mult).then_inc(cat_f, 1)
                for g in GATED_AT.get(s - S_PAIR - 4, ()):
                    pool.wait_ge(cat_h, g + 1)
                    pool.tensor_tensor(cat_lo[:, g, :], vg[:, g, :], cat_hi[:, g, :].bitcast(F32), ALU.subtract)\
                        .then_inc(cat_l, 1)
            with pool.Fori(7, 17) as i:
                for b in range(3):
                    lo_part(3 * i + b, raw_ab(b), hi_lo_ab(b))
            for s in (51, 52):
                lo_part(s, raw_ab(s), hi_lo_ab(s))

            def lo_phase(start, n, tiles):
                with pool.Fori(0, n // 4) as i:
                    for b in range(4):
                        lo_part(4 * i + (start + b), raw_late(b, tiles), hi_lo_late(b, tiles))

            for b in range(4):
                lo_part(S_FFN0 + b, raw_late(b, KD), hi_lo_late(b, KD, b == 2))
            lo_phase(S_FFN0 + 4, GU_SLOTS - 4, KD)
            lo_phase(S_DN0, DN_SLOTS, HALF)
            p = 0

            def add_product():
                nonlocal p
                i, d = POOL_TAPS[p]
                p += 1
                pool.wait_ge(prod_ready, p)
                if p > 1:
                    pool.wait_ge(prod_added, p - 1)
                if p == C_TAPS:
                    pool.wait_ge(conv[1], TILE1_TAPS)
                if p == 1:
                    pool.wait_ge(tap0_done, 1)
                pool.tensor_tensor(c_acc[:, i, d:T], c_acc[:, i, d:T], prods[:, (p - 1) % PRODS, 0:T - d], ALU.add)\
                    .then_inc(prod_added, 1)

            for q in range(24):
                lo_part(S_CD + q, raw_late(q, KD), hi_lo_late(q, KD))
                for _ in range(2 if q >= POOL_START and p < len(POOL_TAPS) else 0):
                    add_product()
            assert p == len(POOL_TAPS)
            lo_phase(S_CD + 24, CDO_SLOTS + GU_SLOTS - 4, KD)
            lo_phase(S_DN1, DN_SLOTS, HALF)

        @block.scalar
        def _(act):
            def hi_late(s, q, tiles, fills, before=2, middle=False):
                act.wait_ge(raw4[q % 4], fills)
                act.wait_ge(slot_done, s - before + 1)
                act.activation(hi_lo_late(q, tiles, middle)[0], raw_late(q, tiles), ACT.Copy).then_inc(hi_ready, 1)

            def x_hi(k, col):
                gain = vecs[:, col + k:col + k + 1]
                act.activation(xg_hi[:, k, :], xres[:, k, :], ACT.Identity, scale=gain).then_inc(xh_ready, 1)

            def x_square(k, h, m):
                if m >= 2:
                    act.wait_ge(sq_used, m - 1)
                act.activation(sq_buf[:, h, :], xres[:, k, :], ACT.Square).then_inc(sq_ready, 1)

            act.wait_ge(cell_ready, 1)
            act.activation(cell[:], cell[:], ACT.Copy)
            act.wait_ge(vecs_loaded, 16)
            for k in range(KD):
                if k < PIECES:
                    act.wait_ge(first_loaded[k] if k < PIECES - 1 else raw3[0], 16)
                    act.activation(piece(hi_lo_ab(0)[0], k), piece(raw_ab(0), k), ACT.Copy)\
                        .then_inc(first_hi if k < PIECES - 1 else hi_ready, 1)
                act.wait_ge(x_loaded[k], 16)
                x_hi(k, V_AB)
                if k == 4:
                    act.wait_ge(raw3[1], 16)
                    act.activation(hi_lo_ab(1)[0], raw_ab(1), ACT.Copy).then_inc(hi_ready, 1)
            for k in range(KD):
                x_square(k, k % 2, k)
                if k == 3:
                    act.wait_ge(raw3[2], 16)
                    act.activation(hi_lo_ab(2)[0], raw_ab(2), ACT.Copy).then_inc(hi_ready, 1)
            def gelu(j):
                act.wait_ge(a_lin, j + 1)
                dst = vg[:, j, :] if j < 4 else u[:, j - 4, :]
                act.activation(natural(dst), classes(tmp[:, j % 2, :]), ACT.Gelu).then_inc(gelu_done, 1)

            for j in range(A_SLOTS):
                s = j + 2
                if s >= 3:
                    act.wait_ge(raw3[s % 3], 16 * (s // 3 + 1))
                    act.wait_ge(slot_done, s - 2)
                    act.activation(hi_lo_ab(s)[0], raw_ab(s), ACT.Copy).then_inc(hi_ready, 1)
                if j >= 2:
                    gelu(j - 2)
            gelu(A_SLOTS - 2)

            def attention_softmax(j, n):
                act.wait_ge(scores_used, n + 1)
                act.activation(prob[:], sm[:], ACT.Exp, bias=nmax[:, j % 2:j % 2 + 1], scale=-1.0,
                               accum_out=den[:, j % 2:j % 2 + 1]).then_inc(exp_done, 1)

            def probs_out(j, n):
                act.wait_ge(pt_ready, n + 1)
                if j:
                    act.wait_ge(pv_done, n)
                act.activation(prob_t[:], probsT, ACT.Copy).then_inc(pt_out, 1)

            def concat_hi(index, f_count, src):
                act.wait_ge(cat_f, f_count)
                act.activation(cat_hi[:, index, :] if isinstance(index, int) else
                               cat_hi[:, bass.ds(index, 1), :].rearrange("p a t -> p (a t)"),
                               src, ACT.Copy).then_inc(cat_h, 1)

            def pair_stage(st, attn, proj=True):
                for j in range(NB_SLOTS):
                    n = 8 * (st - 1) + j
                    s = S_PAIR + 9 * st + j
                    if attn and j >= 1:
                        probs_out(j - 1, n - 1)
                    if attn and j < 8:
                        attention_softmax(j, n)
                    if not proj and s + 2 >= AB_SLOTS:
                        if j == 7:
                            hi_late(S_FFN0, 0, KD, 16, before=3)
                    else:
                        act.wait_ge(raw3[(j + 1) % 3], 16 * (3 * st + (S_PAIR + j + 2) // 3 + 1))
                        act.wait_ge(slot_done, s)
                        act.activation(hi_lo_ab(j + 1)[0], raw_ab(j + 1), ACT.Copy).then_inc(hi_ready, 1)
                    if not attn and j == 0:
                        gelu(A_SLOTS - 1)
                    if not attn and j == 2:
                        for c in range(TB):
                            act.wait_ge(ln_factors, 2)
                            act.activation(vg[:, c, :], ps[:, SC + c, :], ACT.Identity, scale=ln_scale[:, c:c + 1],
                                           bias=ln_shift[:, c:c + 1]).then_inc(ln_ready, 1)
                    if not attn:
                        for g in GATED_AT.get(j - 2, ()):
                            concat_hi(g, g + 1, vg[:, g, :])
                    if proj:
                        if j == (8 if attn else 4):
                            if attn:
                                act.wait_ge(scores_ready, 8 * st)
                            act.wait_ge(q0_ready, st + 1)
                            act.activation(qk_hi[:], qk_next[:, 0:2, :], ACT.Copy).then_inc(qk_hi_ready, 1)
                        act.wait_ge(slot_done, s + 1)
                        bank = MISC if attn and j == 8 else j % 2
                        if j < 6:
                            if attn:
                                act.wait_ge(qk_cur_ready, 4 * st)
                                act.wait_ge(qk_lo_ready, st)
                            act.activation(qk_next[:, j, :], ps[:, bank, :], ACT.Copy)
                            if j >= 2:
                                act.wait_ge(misc_ready, misc_squares(st, j // 2 - 1, j % 2, attn) + 1)
                            elif attn:
                                act.wait_ge(misc_ready, misc_base(st, attn))
                            else:
                                act.wait_ge(sq_used, KD)
                            act.activation(sq_buf[:, j % 2, :], ps[:, bank, :], ACT.Square).then_inc(qkv_used, 1)
                        else:
                            if j == 6 and attn:
                                act.wait_ge(misc_ready, misc_base(st, attn) + 3)
                            act.activation(v_raw[:, j - 6, :], ps[:, bank, :], ACT.Copy).then_inc(qkv_used, 1)
                if attn:
                    concat_hi(st + 3, 4 + st, tmp[:, 0, :])

            pair_stage(0, False)
            with act.Fori(1, PAIRS) as st:
                pair_stage(st, True)
            pair_stage(PAIRS, True, proj=False)

            hi_late(S_FFN0 + 1, 1, KD, 16, before=3)
            for k in range(KD):
                act.wait_ge(out_used, KD + k + 1)
                x_hi(k, V_F0)
                x_square(k, k % 2, KD + k)
                if k == KD - 2:
                    hi_late(S_FFN0 + 2, 2, KD, 16, before=3, middle=True)

            def gate_up(s0, q0, f0, next_tiles):
                if q0:
                    hi_late(s0 + 2, 2, KD, 16 * (q0 // 4 + 1))

                def body(i, last, first=False):
                    for h in range(2):
                        f = 2 * i + (f0 + h)
                        for e in range(2):
                            b = 2 * h + e + 3
                            tiles = next_tiles if last and b >= 4 else KD
                            hi_late(4 * i + (s0 + b), b % 4, tiles, 16 * (i + (q0 // 4 + b // 4 + 1)))
                            if e == (1 if first and h == 0 else 0):
                                act.wait_ge(lin_ready, f + 1)
                                act.activation(g_act[:, 0, :], tmp[:, 0, :], ACT.Silu).then_inc(silu_done, 1)
                                act.wait_ge(h_f, f + 1)
                                dst = h_hi[:, f - f0, :] if isinstance(i, int) else \
                                    h_hi[:, bass.ds(2 * i + h, 1), :].rearrange("p a t -> p (a t)")
                                act.activation(dst, g_act[:, 1, :], ACT.Copy).then_inc(h_h, 1)

                n = GU_SLOTS // 4
                body(0, False, first=True)
                with act.Fori(1, n - 1) as i:
                    body(i, False)
                body(n - 1, True)

            def down(s1, q1, col=None, m0=0):
                def body(i, last):
                    for b in range(3, 7):
                        tiles = HALF if b == 3 or not last else KD
                        if b == 3 or not last or col is not None:
                            hi_late(4 * i + (s1 + b), b % 4, tiles, 16 * (i + (q1 // 4 + b // 4 + 1)))
                        if col is not None and b in (3, 5):
                            n = 2 * i + (b - 3) // 2
                            act.wait_ge(dn_used, n + 1)
                            x_hi(n, col)
                            x_square(n, (b - 3) // 2, n + m0)
                        if last and b == 5:
                            break

                for i in range(DN_SLOTS // 4):
                    body(i, i == DN_SLOTS // 4 - 1)

            gate_up(S_FFN0, 0, 0, HALF)
            down(S_DN0, GU_SLOTS, V_CD, 2 * KD)
            q_cd = GU_SLOTS + DN_SLOTS

            n_cat = 0
            products = [0]

            def first_tap(i):
                w = V_CW + i * C_TAPS + C_TAPS - 1
                act.wait_ge(c_ready, i + 1)
                act.activation(c_acc[:, i, :], c_in[:, i, :], ACT.Identity, scale=vecs[:, w:w + 1],
                               bias=vecs[:, V_CB + i:V_CB + i + 1]).then_inc(tap0_done, 1)

            def pool_tap():
                p = products[0]
                if p == len(POOL_TAPS):
                    return
                i, d = POOL_TAPS[p]
                w = V_CW + i * C_TAPS + C_TAPS - 1 - d
                if p >= PRODS:
                    act.wait_ge(prod_added, p - PRODS + 1)
                act.activation(prods[:, p % PRODS, :], c_in[:, i, :], ACT.Identity, scale=vecs[:, w:w + 1])\
                    .then_inc(prod_ready, 1)
                products[0] += 1

            for q in range(CD_SLOTS + CDO_SLOTS):
                hi_late(S_CD + q + 2, (q + 2) % 4, KD, 16 * ((q_cd + q + 2) // 4 + 1))
                if 2 <= q <= 8 and q % 2 == 0:
                    i = q // 2 - 1
                    act.wait_ge(cd_used, 2 * i + 2)
                    act.activation(c_sig[:, i % 2, :], c_gate[:, i % 2, :], ACT.Sigmoid).then_inc(cgate_act, 1)
                    first_tap(i)
                if 2 <= q < 21:
                    for _ in range(2):
                        pool_tap()
                if q >= 24:
                    for k in (2 * (q - 24), 2 * (q - 24) + 1):
                        act.wait_ge(cd_used, 28 + k + 1)
                        x_hi(k, V_F1)
                        x_square(k, k % 2, 3 * KD + 4 + k)
                if 8 <= q < 20 and (q - 8) % 3 == 2:
                    act.wait_ge(cd_used, q + 1)
                    act.activation(ccat_hi[:, 4 + n_cat, :], d_out[:, n_cat % 2, :], ACT.Copy).then_inc(ccat_h, 1)
                    n_cat += 1
                if q < 20 and (q - 8) % 3 == 1 and q >= 8:
                    i = (q - 8) // 3
                    w = V_DW + i * D_TAPS + D_TAPS - 1
                    act.wait_ge(cd_used, q + 1)
                    act.activation(d_z[:, i % 2, :], d_y[:, i % 2, :], ACT.Identity, scale=vecs[:, w:w + 1])\
                        .then_inc(dz_ready, 1)
                if q == 20:
                    for i in range(4):
                        act.wait_ge(xc_ready, i + 1)
                        act.wait_ge(sq_used, 3 * KD + i - 1)
                        act.activation(sq_buf[:, i % 2, :], c_acc[:, i, :], ACT.Square).then_inc(sq_ready, 1)
                if q == 22:
                    for i in range(4):
                        act.wait_ge(cn_ready, i + 1)
                        act.activation(c_in[:, i, :], c_acc[:, i, :], ACT.Silu, scale=vecs[:, V_LG + i:V_LG + i + 1],
                                       bias=vecs[:, V_LB + i:V_LB + i + 1]).then_inc(csilu_done, 1)
                        act.wait_ge(csilu_done, i + 1)
                        act.activation(ccat_hi[:, i, :], c_in[:, i, :], ACT.Copy).then_inc(ccat_h, 1)

            q_f1 = q_cd + CD_SLOTS + CDO_SLOTS
            gate_up(S_FFN1, q_f1, NF, HALF)
            down(S_DN1, q_f1 + GU_SLOTS)

        @block.tensor
        def _(pe):
            def passes(out_, hi, lo, t, m_hi, m_lo, first, last):
                w_hi, w_lo = hi[:, t * P:(t + 1) * P], lo[:, t * P:(t + 1) * P]
                pe.matmul(out_, w_hi, m_hi, start=first, stop=False)
                pe.matmul(out_, w_hi, m_lo, start=False, stop=False)
                return pe.matmul(out_, w_lo, m_hi, start=False, stop=last)

            def project(s, hi_lo, bank, act_hi, act_lo, kts=range(KD), ready=None):
                if not (isinstance(s, int) and s == 0):
                    pe.wait_ge(lo_ready, s + 1)
                for t, k in enumerate(kts):
                    if isinstance(s, int) and s == 0 and t % (KD // PIECES) == 0:
                        c = t * PIECES // KD
                        pe.wait_ge(*((first_lo, c + 1) if c < PIECES - 1 else (lo_ready, 1)))
                    if ready is not None:
                        pe.wait_ge(ready[0], ready[1] + k + 1)
                    last = passes(ps[:, bank, :], *hi_lo, t, act_hi[:, k, :], act_lo[:, k, :], t == 0,
                                  t == len(kts) - 1)
                last.then_inc(slot_done, 1)

            def norm_sums(which, mean_col):
                pe.wait_ge(sq_used, (8, 16, 24, 28, 36)[which - 1])
                for r in range(TB):
                    last = pe.matmul(ps[:, STAT, r:r + 1], sq_acc[:, r * P:(r + 1) * P],
                                     consts[:, mean_col:mean_col + 1], start=True, stop=True)
                last.then_inc(stat_ready, 1)

            def norm_spread(which):
                pe.wait_ge(rstd_tok, which)
                for r in range(TB):
                    last = pe.transpose(ps[:, BC, r * P:(r + 1) * P],
                                        rstd_t[:, r:r + 1].to_broadcast([P, P]), ident)
                last.then_inc(bc_ready, 1)

            def first_two(s, places, banks, base):
                def some(b, ks):
                    for k in ks:
                        if b == 0:
                            pe.wait_ge(xg_ready, base + k + 1)
                        last = passes(ps[:, banks[b], :], *places[b], k, xg_hi[:, k, :], xg_lo[:, k, :], k == 0,
                                      k == KD - 1)
                    if ks[-1] == KD - 1:
                        last.then_inc(slot_done, 1)

                pe.wait_ge(lo_ready, s + 1)
                some(0, range(KD - 1))
                pe.wait_ge(lo_ready, s + 2)
                some(1, range(2))
                some(0, range(KD - 1, KD))
                some(1, range(2, KD))

            for j in range(A_SLOTS):
                if j >= 5:
                    pe.wait_ge(a_lin, j - 4)
                project(j, hi_lo_ab(j), j % 5, xg_hi, xg_lo, ready=(xg_ready, 0) if j == 0 else None)
                if j == 1:
                    pe.wait_ge(const_loaded, 16)
                    norm_sums(1, C_1024)
                if j == 2:
                    norm_spread(1)
                if j == 4:
                    pe.wait_ge(sguw_masked, 1)
                    pe.matmul(ps[:, WSUM, :], consts[:, C_ONES:C_ONES + P],
                              sguw[:].rearrange("p g t -> p (g t)"), start=True, stop=True).then_inc(wsum_ready, 1)

            def score(j, n):
                h, r = divmod(j, TB)
                rows_ = slice(64 * h, 64 * h + 64)
                cls = slice(r * P, (r + 1) * P)
                if j:
                    pe.wait_ge(scores_used, n)
                q_hi, q_lo = (z[rows_, 0, cls] for z in (qk_hi, qk_lo))
                k_hi, k_lo = (z[rows_, 1, :] for z in (qk_hi, qk_lo))
                pe.matmul(scores[:, 0:T], q_hi, k_hi, start=True, stop=False)
                pe.matmul(scores[:, 0:T], q_hi, k_lo, start=False, stop=False)
                pe.matmul(scores[:, 0:T], q_lo, k_hi, start=False, stop=True)
                pe.matmul(scores[:, T:T + P], qk_cur[rows_, 0, cls], qk_cur[rows_, 1, cls], start=True, stop=True)
                pe.matmul(scores[:, T + P:KEYS], qk_cur[rows_, 2, cls], qk_cur[rows_, 3, cls], start=True, stop=True)\
                    .then_inc(scores_ready, 1)

            def turn(n):
                pe.wait_ge(probs_ready, n + 1)
                for c in range(KEYS // P):
                    last = pe.transpose(probsT[:, c * P:(c + 1) * P], prob[:, c * P:(c + 1) * P], ident)
                last.then_inc(pt_ready, 1)

            def weigh(j, n):
                h, r = divmod(j, TB)
                pe.wait_ge(pt_out, n + 1)
                blocks = [(0, c) for c in range(TB)] + [(1, r), (2, r)]
                for c, (g, blk) in enumerate(blocks):
                    last = pe.matmul(ps[64 * h:64 * h + 64, OB, r * P:(r + 1) * P],
                                     v_cur[:, g, blk, 64 * h:64 * h + 64], prob_t[:, c * P:(c + 1) * P],
                                     start=(c == 0), stop=(c == len(blocks) - 1))
                last.then_inc(pv_done, 1)

            def misc_done_before(k):
                pe.wait_ge(misc_used, k)

            def misc_free(k, attn):
                if attn or k >= 2:
                    misc_done_before(k if attn else k - 1)

            def turn_v(g, st, k):
                misc_done_before(k)
                if g == 0:
                    pe.wait_ge(qkv_used, 9 * st)
                for r in range(TB):
                    last = pe.transpose(ps[:, MISC, r * P:(r + 1) * P], v_raw[:, g, r * P:(r + 1) * P], ident)
                last.then_inc(misc_ready, 1)

            def turn_squares(b, t, st, attn):
                k = misc_squares(st, b, t, attn)
                misc_free(k, attn)
                pe.wait_ge(qkv_used, 9 * st + (2 * b + t + 1))
                for r in range(TB):
                    last = pe.transpose(ps[:, misc_bank(t, attn), r * P:(r + 1) * P],
                                        sq_buf[:, t, r * P:(r + 1) * P], ident)
                last.then_inc(misc_ready, 1)

            def head_spread(b, t, st, attn):
                misc_free(misc_squares(st, b, t, attn) + 2, attn)
                pe.wait_ge(rq_ready, 3 * st + b + 1)
                for r in range(TB):
                    c = (t * TB + r) * 2
                    last = pe.transpose(ps[:, misc_bank(t, attn), r * P:(r + 1) * P],
                                        wide[:, c * 64:(c + 2) * 64], ident)
                last.then_inc(misc_ready, 1)

            def pair_stage(st, attn, proj=True):
                base = misc_base(st, attn)
                nv = 3 if attn else 0
                for j in range(NB_SLOTS):
                    n = 8 * (st - 1) + j
                    s = S_PAIR + 9 * st + j
                    if attn and j < 8:
                        if j == 0:
                            pe.wait_ge(qk_cur_ready, 4 * st)
                            pe.wait_ge(qk_lo_ready, st)
                            pe.wait_ge(cat_f, 4)
                        score(j, n)
                    if attn and j >= 1:
                        if j == 1:
                            pe.wait_ge(cat_l, 4)
                        turn(n - 1)
                    if attn and j == 0:
                        turn_v(0, st, base)
                    if attn and j == 1:
                        turn_v(2, st, base + 2)
                    if proj:
                        if attn and j in (2, 4, 6):
                            turn_squares(j // 2 - 1, 1, st, attn)
                        if attn and j in (3, 5, 7):
                            head_spread((j - 3) // 2, 1, st, attn)
                        if attn and j == 8:
                            misc_done_before(base + nv + 12)
                        elif j >= 2:
                            pe.wait_ge(qkv_used, 9 * st + j - 1)
                        elif attn:
                            pe.wait_ge(qkv_used, 9 * st - 3 + j + 1)
                        else:
                            pe.wait_ge(a_lin, 6 + j)
                        project(s, hi_lo_ab(S_PAIR + j), MISC if attn and j == 8 else j % 2, xg_hi, xg_lo)
                    if not proj and j in (7, 8):
                        if j == 7:
                            pe.wait_ge(lo_ready, s + 1)
                            pe.wait_ge(out_used, j - 1)
                        out_part(range(3) if j == 7 else range(3, 5))
                    if not proj and j < 7:
                        if j < 2:
                            pe.wait_ge(qkv_used, 9 * st)
                        else:
                            pe.wait_ge(out_used, j - 1)
                        project(s, hi_lo_ab(S_PAIR + j), j % 2, cat_hi, cat_lo, kts=range(KD - 1),
                                ready=(cat_l, 0) if j == 0 else None)
                    if proj and not attn and j == 0:
                        pe.wait_ge(gelu_done, 4)
                        pe.wait_ge(a_lin, A_SLOTS)
                        pe.wait_ge(sgu_bias_ready, 4)
                        for c in range(TB):
                            for g in range(4):
                                last = pe.transpose(ps[:, SC + c, g * P:(g + 1) * P],
                                                    vg[:, g, c * P:(c + 1) * P], ident)
                            last.then_inc(vt_ready, 1)
                    if attn and j == 0:
                        turn_v(1, st, base + 1)
                    if proj and attn and j in (1, 3, 5):
                        turn_squares(j // 2, 0, st, attn)
                    if proj and attn and j in (2, 4, 6):
                        head_spread(j // 2 - 1, 0, st, attn)
                    if proj and not attn and j in (2, 4, 6):
                        for t in range(2):
                            turn_squares(j // 2 - 1, t, st, attn)
                    if proj and not attn and j in (3, 5, 7):
                        for t in range(2):
                            head_spread((j - 3) // 2, t, st, attn)
                    if proj and not attn and j == 3:
                        pe.wait_ge(ln_ready, 4)
                        for g in range(4):
                            for c in range(TB):
                                last = pe.matmul(ps[:, SC + g, c * P:(c + 1) * P], vg[:, c, g * P:(g + 1) * P],
                                                 sguw[:, g, :], start=True, stop=True)
                            last.then_inc(mix_ready, 1)
                    if attn and j >= 1:
                        if j == 1:
                            pe.wait_ge(misc_used, base + 3)
                            pe.wait_ge(cat_f, 3 + st)
                        weigh(j - 1, n - 1)

            def out_part(ks):
                for k in ks:
                    last = passes(ps[:, 1, :], *hi_lo_ab(S_PAIR + 7), k, cat_hi[:, k, :], cat_lo[:, k, :], k == 0,
                                  k == KD - 2)
                return last

            pair_stage(0, False)
            with pe.Fori(1, PAIRS) as st:
                pair_stage(st, True)
            pair_stage(PAIRS, True, proj=False)
            out_part(range(5, KD - 1)).then_inc(slot_done, 1)
            s = AB_SLOTS - 1
            pe.wait_ge(lo_ready, s + 1)
            pe.wait_ge(cat_l, 8)
            hi, lo = hi_lo_ab(s)
            for n in range(KD + 4):
                if n < KD:
                    if n >= 4:
                        pe.wait_ge(out_used, KD + n - 3)
                    last = passes(ps[:, SC + n % 4, :], hi, lo, n, cat_hi[:, KD - 1, :], cat_lo[:, KD - 1, :],
                                  True, True)
                    last.then_inc(out_ready if n < KD - 1 else slot_done, 1)
                if n >= 4:
                    k = n - 4
                    if k == 0:
                        pe.wait_ge(out_used, KD)
                        pe.wait_ge(lo_ready, S_FFN0 + 2)
                    pe.wait_ge(xg_ready, KD + k + 1)
                    for b in range(2):
                        last = passes(ps[:, b, :], *hi_lo_late(b, KD), k, xg_hi[:, k, :], xg_lo[:, k, :], k == 0,
                                      k == KD - 1)
                        if k == KD - 1:
                            last.then_inc(slot_done, 1)

            def gate_up(s0, q0, f0, which):
                def body(i, first):
                    for b in range(4):
                        if not first:
                            pe.wait_ge(up_used if b % 2 else lin_ready, 2 * i + (f0 + b // 2 - 1))
                        elif b == 2:
                            pe.wait_ge(*((out_used, 2 * KD) if which == 2 else (cd_used, CD_SLOTS + 2 * CDO_SLOTS)))
                        elif b == 0 and which != 2:
                            pe.wait_ge(cd_used, CD_SLOTS + 2 * CDO_SLOTS - 4)
                            first_two(s0, [hi_lo_late(q, KD) for q in (0, 1)], (0, 1), 3 * KD)
                        if not (first and b < 2):
                            project(4 * i + (s0 + b), hi_lo_late(b, KD, first and which == 2 and b == 2), b,
                                    xg_hi, xg_lo)
                        if first and b == 1:
                            norm_sums(norm_index[which], C_1024)
                        if first and b == 2:
                            norm_spread(norm_index[which])

                body(0, True)
                with pe.Fori(1, GU_SLOTS // 4) as i:
                    body(i, False)

            norm_index = {2: 2, 4: 5}

            def down(s1, f0, n0):
                def body(i, first):
                    for b in range(4):
                        bank = 4 + b // 2
                        hi, lo = hi_lo_late(b, HALF)
                        s_ = 4 * i + (s1 + b)
                        pe.wait_ge(lo_ready, s_ + 1)
                        if not first and b % 2 == 0:
                            pe.wait_ge(dn_used, 2 * i + (n0 + b // 2 - 1))
                        for t in range(HALF):
                            k = (b % 2) * HALF + t
                            if first and b < 2:
                                pe.wait_ge(h_ready, f0 + k + 1)
                            last = passes(ps[:, bank, :], hi, lo, t, h_hi[:, k, :], h_lo[:, k, :], k == 0,
                                          k == NF - 1)
                        last.then_inc(slot_done, 1)

                body(0, True)
                with pe.Fori(1, DN_SLOTS // 4) as i:
                    body(i, False)

            gate_up(S_FFN0, 0, 0, 2)
            down(S_DN0, 0, 0)

            e = 0
            first_two(S_CD, [hi_lo_late(q, KD) for q in (0, 1)], (0, 1), 2 * KD)
            for q in range(CD_SLOTS):
                if q == 2:
                    pe.wait_ge(dn_used, KD)
                if e >= 6:
                    pe.wait_ge(cd_used, e - 5)
                if q >= 2:
                    project(S_CD + q, hi_lo_late(q, KD), e % 6, xg_hi, xg_lo)
                e += 1
                if q == 1:
                    norm_sums(3, C_1024)
                if q == 2:
                    norm_spread(3)

            def out_slot(m, half):
                nonlocal e
                q = CD_SLOTS + m
                hi, lo = hi_lo_late(q, KD)
                pe.wait_ge(lo_ready, S_CD + q + 1)
                if m % 4 == 0:
                    pe.wait_ge(cd_used, e - 4)
                    for t in range(4):
                        pe.wait_ge(ccat_l, 4 * (1 - half) + t + 1)
                        for n in range(2):
                            last = passes(ps[:, (e + n) % 6, :], hi, lo, 4 * n + t, ccat_hi[:, 4 * half + t, :],
                                          ccat_lo[:, 4 * half + t, :], t == 0, t == 3)
                            if t == 3:
                                last.then_inc(slot_done if n else cdo_ready, 1)
                    e += 2
                    return
                for n in range(2):
                    pe.wait_ge(cd_used, e - 5)
                    for t in range(4):
                        last = passes(ps[:, e % 6, :], hi, lo, 4 * n + t, ccat_hi[:, 4 * half + t, :],
                                      ccat_lo[:, 4 * half + t, :], t == 0, t == 3)
                    last.then_inc(slot_done if n else cdo_ready, 1)
                    e += 1

            def channel_mean():
                for i in range(1, 4):
                    pe.wait_ge(conv[i], DVE_TAPS[i])
                pe.wait_ge(prod_added, len(POOL_TAPS))
                for i in range(4):
                    last = pe.matmul(ps[:, BC, :], consts[:, C_AVG:C_AVG + P], c_acc[:, i, :], start=(i == 0),
                                     stop=(i == 3))
                last.then_inc(mean_ready, 1)

            out_slot(0, 1)
            channel_mean()
            out_slot(1, 1)
            norm_sums(4, C_512)
            out_slot(2, 1)
            norm_spread(4)
            out_slot(3, 1)
            for m in range(4, 8):
                out_slot(m, 0)

            gate_up(S_FFN1, 0, NF, 4)
            down(S_DN1, NF, KD)

        @block.vector
        def _(v):
            order = [0, 0]

            def link(ins, fence=True):
                order[1] += 1
                ins.then_inc(dve, 1)
                if fence:
                    v.wait_ge(dve, order[0] + order[1])

            def gate():
                link(v.memset(gate_cell[:], 0.0), fence=False)

            def rsqrt(n):
                m, y, t, h = (z[:, 0:n] for z in (st_m, st_y, st_t, st_h))
                link(v.tensor_scalar(t.bitcast(I32), m.bitcast(I32), 1, None, ALU.logical_shift_right), fence=False)
                link(v.tensor_scalar(h, m, -0.5, None, ALU.mult))
                link(v.tensor_scalar(y.bitcast(I32), t.bitcast(I32), -1.0, MAGIC, ALU.mult, ALU.add))
                for _ in range(3):
                    link(v.tensor_tensor(t, y, y, ALU.mult))
                    link(v.tensor_tensor(t, t, h, ALU.mult))
                    link(v.scalar_tensor_tensor(out=y, in0=t, scalar=1.5, in1=y, op0=ALU.add, op1=ALU.mult))

            def x_lo(k, col, count):
                gain = vecs[:, col + k:col + k + 1]
                v.wait_ge(xh_ready, count)
                v.scalar_tensor_tensor(out=xg_lo[:, k, :], in0=xres[:, k, :], scalar=gain,
                                       in1=xg_hi[:, k, :].bitcast(F32), op0=ALU.mult, op1=ALU.subtract)\
                    .then_inc(xg_ready, 1)

            def norm_finish(which, spread=True):
                v.wait_ge(stat_ready, which)
                link(v.tensor_scalar(st_m[:, 0:TB], ps[:, STAT, 0:TB], EPS, None, ALU.add))
                rsqrt(TB)
                v.tensor_copy(rstd_t[:], st_y[:, 0:TB]).then_inc(rstd_tok, 1)
                if spread:
                    v.wait_ge(bc_ready, which)
                    v.tensor_copy(rstd_b, ps[:, BC, :]).then_inc(rstd_ready, 1)
                    v.wait_ge(rstd_ready, rstd_count[which])

            rstd_count = {1: 1, 2: 2, 3: 3, 5: 4}

            def add_square(h, m, restart=False):
                v.wait_ge(sq_ready, m + 1)
                if restart:
                    v.tensor_copy(sq_acc, sq_buf[:, h, :]).then_inc(sq_used, 1)
                else:
                    v.wait_ge(sq_used, m)
                    v.tensor_tensor(sq_acc, sq_acc, sq_buf[:, h, :], ALU.add).then_inc(sq_used, 1)

            def scaled(dst, bank):
                return v.tensor_tensor(dst, ps[:, bank, :], rstd_b, ALU.mult)

            v.wait_ge(vecs_loaded, 16)
            for k in range(KD):
                x_lo(k, V_AB, k + 1)
            for k in range(KD):
                add_square(k % 2, k, restart=(k == 0))
            norm_finish(1)
            link(v.tensor_tensor(rstd_t2[:], rstd_t[:], rstd_t[:], ALU.mult))
            for j in range(A_SLOTS):
                v.wait_ge(slot_done, j + 1)
                if j >= 2:
                    v.wait_ge(gelu_done, j - 1)
                scaled(tmp[:, j % 2, :], j % 5).then_inc(a_lin, 1)
            v.wait_ge(wsum_ready, 1)
            v.wait_ge(a_loaded, 32)
            for g in range(4):
                v.scalar_tensor_tensor(out=gate_bias[:, g, :], in0=ps[:, WSUM, g * P:(g + 1) * P],
                                       scalar=vecs[:, V_SB + g:V_SB + g + 1], in1=sgu_bias[:, g, :],
                                       op0=ALU.mult, op1=ALU.add).then_inc(sgu_bias_ready, 1)
            v.wait_ge(sgu_bias_ready, 4)

            def scores_to_softmax(j, n):
                v.wait_ge(masks_loaded[j % TB], 16)
                v.wait_ge(scores_ready, n + 1)
                gate()
                v.tensor_tensor_reduce(out=sm[:], in0=scores, in1=masks[j % TB], scale=-0.125, scalar=BIG,
                                       op0=ALU.add, op1=ALU.min, accum_out=nmax[:, j % 2:j % 2 + 1])\
                    .then_inc(scores_used, 1)

            def normalise(j, n):
                v.wait_ge(exp_done, n + 1)
                link(v.reciprocal(rden[:, j % 2:j % 2 + 1], den[:, j % 2:j % 2 + 1]))
                v.tensor_scalar(prob[:], prob[:], rden[:, j % 2:j % 2 + 1], None, ALU.mult).then_inc(probs_ready, 1)

            def v_out(g, k):
                v.wait_ge(misc_ready, k + 1)
                v.tensor_tensor(v_cur[:, g, :, :], ps[:, MISC, :].rearrange("p (r c) -> p r c", r=TB),
                                rstd_t[:, :].unsqueeze(2).to_broadcast([P, TB, P]), ALU.mult).then_inc(misc_used, 1)

            def sum_squares(b, t, st, attn):
                k = misc_squares(st, b, t, attn)
                v.wait_ge(misc_ready, k + 1)
                v.tensor_reduce(st_m[:, 8 * t:8 * t + 8],
                                ps[:, misc_bank(t, attn), :].rearrange("p (r h d) -> p (r h) d", r=TB, h=2),
                                mybir.AxisListType.X, ALU.add).then_inc(misc_used, 1)

            def head_factors(b, st, attn):
                v.wait_ge(misc_used, misc_squares(st, b, 1, attn) + 1)
                for t in range(2):
                    m4 = st_m[:, 8 * t:8 * t + 8].rearrange("p (r h) -> p r h", r=TB)
                    link(v.tensor_tensor(m4, m4, rstd_t2[:, :].unsqueeze(2).to_broadcast([P, TB, 2]), ALU.mult),
                         fence=(t == 1))
                link(v.tensor_scalar(st_m[:, 0:16], st_m[:, 0:16], 1 / HEAD, EPS, ALU.mult, ALU.add))
                rsqrt(16)
                y4 = st_y[:, 0:16].rearrange("p (t r h) -> p t r h", t=2, r=TB)
                for t in range(2):
                    ins = v.tensor_tensor(wide[:].rearrange("p (t r h d) -> p t r h d", t=2, r=TB, h=2)[:, t],
                                          y4[:, t, :, :].unsqueeze(3).to_broadcast([P, TB, 2, 64]),
                                          rstd_t[:, :].unsqueeze(2).unsqueeze(3).to_broadcast([P, TB, 2, 64]), ALU.mult)
                ins.then_inc(rq_ready, 1)

            def head_scale(b, t, st, attn):
                tile_ = 2 * b + t
                k = misc_squares(st, b, t, attn) + 2
                v.wait_ge(misc_ready, k + 1)
                v.scalar_tensor_tensor(out=qk_next[:, tile_, :], in0=qk_next[:, tile_, :],
                                       scalar=vecs[:, V_QK + tile_:V_QK + tile_ + 1],
                                       in1=ps[:, misc_bank(t, attn), :],
                                       op0=ALU.mult, op1=ALU.mult).then_inc(misc_used, 1)
                v.wait_ge(misc_used, k + 1)

            half_turn = [i + 8 if i < 8 else i - 8 if i < 16 else i for i in range(32)]

            def rotate(b, direct, st, attn):
                both = qk_next[:, 2 * b:2 * b + 2, :]
                v.wait_ge(dve, order[0] + order[1])
                if not attn and b == 2:
                    v.wait_ge(qk_cur_ready, 2 * (b - 1))
                gate()
                link(v.stream_shuffle(tmp[:], both, half_turn), fence=False)
                link(v.tensor_tensor(both, both, rope[:, 0:1, :].to_broadcast([P, 2, T]), ALU.mult), fence=False)
                v.wait_ge(dve, order[0] + (order[1] - 1))
                link(v.tensor_tensor(tmp[:], tmp[:], rope[:, 1:2, :].to_broadcast([P, 2, T]), ALU.mult))
                if b == 0:
                    v.tensor_tensor(both, both, tmp[:], ALU.add).then_inc(q0_ready, 1)
                    v.wait_ge(q0_ready, st + 1)
                elif direct:
                    v.tensor_tensor(qk_cur[:, 2 * b - 2:2 * b, :], both, tmp[:], ALU.add).then_inc(qk_cur_ready, 2)
                else:
                    link(v.tensor_tensor(both, both, tmp[:], ALU.add))

            def attention_out(st, proj):
                v.wait_ge(pv_done, 8 * st)
                v.wait_ge(qk_cur_ready, 4 * st + (4 if proj else 0))
                v.tensor_copy(natural(tmp[:, 0, :]), classes(ps[:, OB, :])).then_inc(cat_f, 1)
                v.wait_ge(cat_h, 4 + st)
                dyn = (slice(None), bass.ds(st + 3, 1), slice(None))
                if isinstance(st, int):
                    hi, lo = cat_hi[:, st + 3, :], cat_lo[:, st + 3, :]
                else:
                    hi, lo = (z[dyn].rearrange("p a t -> p (a t)") for z in (cat_hi, cat_lo))
                v.tensor_tensor(lo, tmp[:, 0, :], hi.bitcast(F32), ALU.subtract).then_inc(cat_l, 1)
                v.wait_ge(cat_l, 4 + st)

            def pair_stage(st, attn, proj=True):
                base = misc_base(st, attn)
                nv = 3 if attn else 0
                for j in range(NB_SLOTS):
                    n = 8 * (st - 1) + j
                    if attn and j < 8:
                        scores_to_softmax(j, n)
                    if attn and j == 0:
                        v_out(0, base)
                    if attn and j == 1:
                        v_out(2, base + 2)
                    if proj and not attn and j == 0:
                        gmlp_norm()
                    if proj and attn:
                        if j in (2, 4, 6):
                            sum_squares(j // 2 - 1, 1, st, attn)
                            head_factors(j // 2 - 1, st, attn)
                        if j in (3, 5, 7):
                            head_scale((j - 3) // 2, 1, st, attn)
                        if j < 8:
                            normalise(j, n)
                        if j in (3, 5, 7):
                            rotate((j - 3) // 2, j == 7, st, attn)
                        if j == 0:
                            v_out(1, base + 1)
                        if j in (1, 3, 5):
                            sum_squares(j // 2, 0, st, attn)
                        if j in (2, 4, 6):
                            head_scale(j // 2 - 1, 0, st, attn)
                    elif attn:
                        if j < 8:
                            normalise(j, n)
                        if j == 0:
                            v_out(1, base + 1)
                    else:
                        if j in (2, 4, 6):
                            for t in range(2):
                                sum_squares(j // 2 - 1, t, st, attn)
                            head_factors(j // 2 - 1, st, attn)
                        if j in (3, 5, 7):
                            for t in range(2):
                                head_scale((j - 3) // 2, t, st, attn)
                            rotate((j - 3) // 2, True, st, attn)
                    if not attn:
                        for g in GATED_AT.get(j, ()):
                            gmlp_gate(g)
                    if not proj and j < 7:
                        v.wait_ge(slot_done, S_PAIR + 9 * st + j + 1)
                        if j == 0:
                            v.wait_ge(xnat_loaded, 16)
                        v.tensor_tensor(xres[:, j, :], xres[:, j, :], ps[:, j % 2, :], ALU.add).then_inc(out_used, 1)
                if proj and attn:
                    v.tensor_copy(qk_cur[:, 0:2, :], qk_next[:, 2:4, :]).then_inc(qk_cur_ready, 2)
                    v.wait_ge(qk_hi_ready, st + 1)
                    v.tensor_tensor(qk_lo[:], qk_next[:, 0:2, :], qk_hi[:].bitcast(F32), ALU.subtract)\
                        .then_inc(qk_lo_ready, 1)
                if attn:
                    attention_out(st, proj)

            def gmlp_norm():
                v.wait_ge(vt_ready, 4)
                v.wait_ge(gelu_done, A_SLOTS)
                for c in range(TB):
                    link(v.bn_stats(bn[:, c, :], ps[:, SC + c, :]), fence=(c == TB - 1))
                for c in range(TB):
                    link(v.bn_aggr(mv[:, c, :], bn[:, c, :]), fence=(c == TB - 1))
                link(v.tensor_scalar(st_m[:, 0:TB], mv[:, :, 1], EPS, None, ALU.add))
                rsqrt(TB)
                v.tensor_copy(ln_scale[:], st_y[:, 0:TB]).then_inc(ln_factors, 1)
                v.scalar_tensor_tensor(out=ln_shift[:], in0=mv[:, :, 0], scalar=-1.0, in1=st_y[:, 0:TB],
                                       op0=ALU.mult, op1=ALU.mult).then_inc(ln_factors, 1)

            def gmlp_gate(g):
                v.wait_ge(mix_ready, 4)
                v.wait_ge(gelu_done, A_SLOTS)
                dst = vg[:, g, :]
                bias = gate_bias[:, g:g + 1, :].to_broadcast([P, TB, P])
                v.scalar_tensor_tensor(out=dst.rearrange("p (c t) -> p c t", c=TB),
                                       in0=ps[:, SC + g, :].rearrange("p (c t) -> p c t", c=TB),
                                       scalar=vecs[:, V_SG + g:V_SG + g + 1], in1=bias, op0=ALU.mult,
                                       op1=ALU.add).then_inc(gate_ready, 1)

            v.wait_ge(rope_loaded, 16)
            pair_stage(0, False)
            start = order[1]
            per = LOOP_STEPS
            with v.Fori(1, PAIRS) as st:
                order[0], order[1] = (st - 1) * per + start, 0
                pair_stage(st, True)
                assert order[1] == per, order[1]
            order[0], order[1] = 0, start + 3 * per
            pair_stage(PAIRS, True, proj=False)
            v.wait_ge(slot_done, AB_SLOTS - 1)
            v.tensor_tensor(xres[:, 7, :], xres[:, 7, :], ps[:, 1, :], ALU.add).then_inc(out_used, 1)
            for n in range(KD):
                v.wait_ge(*((out_ready, n + 1) if n < KD - 1 else (slot_done, AB_SLOTS)))
                v.wait_ge(out_used, n + 1)
                v.tensor_tensor(xres[:, n, :], xres[:, n, :], ps[:, SC + n % 4, :], ALU.add).then_inc(out_used, 1)
                if n >= 1:
                    x_lo(n - 1, V_F0, KD + n)
                    add_square((n - 1) % 2, KD + n - 1, restart=(n == 1))
            x_lo(KD - 1, V_F0, 2 * KD)
            add_square((KD - 1) % 2, 2 * KD - 1)

            def gate_up(s0, f0):
                with v.Fori(0, NF // 2) as i:
                    for h in range(2):
                        f = 2 * i + (f0 + h)
                        v.wait_ge(slot_done, 4 * i + (s0 + 2 * h + 1))
                        scaled(tmp[:, 0, :], 2 * h).then_inc(lin_ready, 1)
                        v.wait_ge(slot_done, 4 * i + (s0 + 2 * h + 2))
                        scaled(tmp[:, 1, :], 2 * h + 1).then_inc(up_used, 1)
                        v.wait_ge(up_used, f + 1)
                        v.wait_ge(silu_done, f + 1)
                        v.tensor_tensor(g_act[:, 1, :], g_act[:, 0, :], tmp[:, 1, :], ALU.mult).then_inc(h_f, 1)
                        v.wait_ge(h_h, f + 1)
                        hi, lo = (z[:, bass.ds(2 * i + h, 1), :].rearrange("p a t -> p (a t)") for z in (h_hi, h_lo))
                        v.tensor_tensor(lo, g_act[:, 1, :], hi.bitcast(F32), ALU.subtract).then_inc(h_ready, 1)

            def down(s1, n0, col=None, m0=0):
                for n in range(KD):
                    v.wait_ge(slot_done, s1 + 2 * n + 2)
                    v.tensor_tensor(xres[:, n, :], xres[:, n, :], ps[:, 4 + n % 2, :], ALU.add).then_inc(dn_used, 1)
                    if col is not None:
                        x_lo(n, col, m0 + n + 1)
                        add_square(n % 2, m0 + n, restart=(n == 0))

            norm_finish(2)
            gate_up(S_FFN0, 0)
            down(S_DN0, 0, V_CD, 2 * KD)
            norm_finish(3)

            taps = [0, 0, 0, 0]
            turn = [0]

            def conv_steps(count, ready):
                while count and any(taps[i] < DVE_TAPS[i] for i in range(1, ready)):
                    turn[0] = turn[0] % (ready - 1) + 1
                    i = turn[0]
                    if taps[i] == DVE_TAPS[i]:
                        continue
                    if taps[i] == 0:
                        v.wait_ge(tap0_done, i + 1)
                    else:
                        v.wait_ge(conv[i], taps[i])
                    taps[i] += 1
                    d = taps[i]
                    w = V_CW + i * C_TAPS + C_TAPS - 1 - d
                    v.scalar_tensor_tensor(out=c_acc[:, i, d:T], in0=c_in[:, i, 0:T - d], scalar=vecs[:, w:w + 1],
                                           in1=c_acc[:, i, d:T], op0=ALU.mult, op1=ALU.add).then_inc(conv[i], 1)
                    count -= 1

            for i in range(4):
                v.wait_ge(slot_done, S_CD + 2 * i + 1)
                scaled(tmp[:, i % 2, :], (2 * i) % 6).then_inc(cd_used, 1)
                conv_steps(CONV_EARLY[0] if i >= 2 else 0, i)
                v.wait_ge(slot_done, S_CD + 2 * i + 2)
                if i >= 2:
                    v.wait_ge(cgate_act, i - 1)
                scaled(c_gate[:, i % 2, :], (2 * i + 1) % 6).then_inc(cd_used, 1)
                conv_steps(CONV_EARLY[1] if i >= 2 else 0, i)
                v.wait_ge(cgate_act, i + 1)
                v.tensor_tensor(c_in[:, i, :], tmp[:, i % 2, :], c_sig[:, i % 2, :], ALU.mult).then_inc(c_ready, 1)
                v.wait_ge(c_ready, i + 1)
                conv_steps(CONV_EARLY[2] if i >= 1 else 0, i + 1)
            link(v.tensor_tensor(rstd_sq[:], rstd_b, rstd_b, ALU.mult))
            for i in range(4):
                b = 8 + 3 * i
                y, z = d_y[:, i % 2, :], d_z[:, i % 2, :]
                v.wait_ge(slot_done, S_CD + b + 1)
                v.tensor_tensor(tmp[:, 0, :], ps[:, b % 6, :], rstd_sq[:], ALU.mult).then_inc(cd_used, 1)
                conv_steps(CONV_STEP[i], 4)
                v.wait_ge(slot_done, S_CD + b + 2)
                v.wait_ge(cd_used, b + 1)
                v.tensor_tensor(y, tmp[:, 0, :], ps[:, (b + 1) % 6, :], ALU.mult).then_inc(cd_used, 1)
                conv_steps(CONV_STEP[i], 4)
                v.wait_ge(dz_ready, i + 1)
                w = V_DW + i * D_TAPS
                for d in (1, 2):
                    if d == 1:
                        v.wait_ge(cd_used, b + 2)
                    link(v.scalar_tensor_tensor(out=z[:, d:T], in0=y[:, 0:T - d], scalar=vecs[:, w + 2 - d:w + 3 - d],
                                                in1=z[:, d:T], op0=ALU.mult, op1=ALU.add))
                link(v.tensor_tensor(z, z, rstd_b, ALU.mult))
                v.wait_ge(slot_done, S_CD + b + 3)
                v.tensor_tensor(d_out[:, i % 2, :], z, ps[:, (b + 2) % 6, :], ALU.mult).then_inc(cd_used, 1)
                conv_steps(CONV_STEP[i] if i < 3 else 0, 4)
                v.wait_ge(ccat_h, i + 1)
                v.tensor_tensor(ccat_lo[:, 4 + i, :], d_out[:, i % 2, :], ccat_hi[:, 4 + i, :].bitcast(F32),
                                ALU.subtract).then_inc(ccat_l, 1)
            e = CD_SLOTS

            def add_out(m):
                nonlocal e
                for n in range(2):
                    if n == 0:
                        v.wait_ge(cdo_ready, m + 1)
                    else:
                        v.wait_ge(slot_done, S_CD + CD_SLOTS + m + 1)
                    t = 2 * (m % 4) + n
                    v.tensor_tensor(xres[:, t, :], xres[:, t, :], ps[:, e % 6, :], ALU.add).then_inc(cd_used, 1)
                    e += 1

            conv_steps(3 * C_TAPS, 4)
            add_out(0)
            v.wait_ge(mean_ready, 1)
            for i in range(4):
                v.tensor_tensor(c_acc[:, i, :], c_acc[:, i, :], ps[:, BC, :], ALU.subtract).then_inc(xc_ready, 1)
            for i in range(4):
                add_square(i % 2, 3 * KD + i, restart=(i == 0))
            add_out(1)
            norm_finish(4, spread=False)
            add_out(2)
            v.wait_ge(bc_ready, 4)
            for i in range(4):
                v.tensor_tensor(c_acc[:, i, :], c_acc[:, i, :], ps[:, BC, :], ALU.mult).then_inc(cn_ready, 1)
            for i in range(4):
                v.wait_ge(ccat_h, 4 + i + 1)
                v.tensor_tensor(ccat_lo[:, i, :], c_in[:, i, :], ccat_hi[:, i, :].bitcast(F32), ALU.subtract)\
                    .then_inc(ccat_l, 1)
            add_out(3)
            for m in range(4, 8):
                v.wait_ge(cd_used, e - 6)
                add_out(m)
                for k in (2 * m - 8, 2 * m - 7):
                    x_lo(k, V_F1, 3 * KD + k + 1)
                for k in (2 * m - 8, 2 * m - 7):
                    add_square(k % 2, 3 * KD + 4 + k, restart=(k == 0))
            norm_finish(5)
            gate_up(S_FFN1, NF)
            down(S_DN1, KD)


TILE1_TAPS = 24
POOL_TAPS = [(0, d) for d in range(1, C_TAPS)] + [(1, d) for d in range(TILE1_TAPS + 1, C_TAPS)]
POOL_START = 4
DVE_TAPS = (0, TILE1_TAPS, C_TAPS - 1, C_TAPS - 1)
LOOP_STEPS = 8 * 2 + 3 * (3 + 12 + 5) - 2
GATED_AT = {4: (0,), 5: (1, 2), 6: (3,)}
CONV_EARLY = (6, 2, 4)
CONV_STEP = (5, 5, 5, 5)


def misc_bank(t, attn):
    return MISC if attn or t == 0 else OB


def misc_base(st, attn):
    return 12 + 15 * (st - 1) if attn else 0


def misc_squares(st, b, t, attn):
    return misc_base(st, attn) + (3 if attn else 0) + 4 * b + t


def _tiles(w, cols, rows):
    import numpy as np
    return np.concatenate([w[k * 128:(k + 1) * 128, c:c + 128] for k, c in zip(rows, cols)], axis=1)


def kernel(**inputs):
    import numpy as np
    import concourse.bacc as _bacc
    from concourse import mybir as _mybir
    from concourse.bass_utils import run_bass_kernel_spmd as _run

    a = {k: np.asarray(v) for k, v in inputs.items()}
    f = np.float32
    k8 = list(range(KD))

    def slot(w, c, ks=k8):
        return _tiles(w, [c] * len(ks), ks)

    w_in, w_out = a["ab_w_in"][0], a["ab_w_out"][0]
    A2 = 1024
    slots = [slot(w_in, 512 + 128 * g) for g in range(4)] + [slot(w_in, 128 * g) for g in range(4)]
    for p in range(PAIRS):
        for g in range(3):
            for which in range(2):
                slots.append(slot(w_in, A2 + which * 1536 + g * 512 + 128 * p))
        for g in range(3):
            slots.append(slot(w_in, A2 + 2 * 1536 + g * 512 + 128 * p))
    for n in range(8):
        slots.append(np.concatenate([slot(w_out, 128 * n, k8[:7]), np.zeros((128, 128), f)], axis=1))
    slots.append(_tiles(w_out, [128 * n for n in range(8)], [7] * 8))

    def gate_up(layer):
        r = []
        for t in range(NF):
            r += [slot(a["ffn_w_gate"][layer], 128 * t), slot(a["ffn_w_up"][layer], 128 * t)]
        return r

    def down(layer):
        w = a["ffn_w_down"][layer]
        return np.stack([slot(w, 128 * n, list(range(HALF * h, HALF * h + HALF))) for n in range(8) for h in range(2)])

    w_ab = np.stack(slots + gate_up(0))
    ci, co = a["cd_w_in"][0], a["cd_w_out"][0]
    cs = []
    for i in range(4):
        cs += [slot(ci, 128 * i), slot(ci, 512 + 128 * i)]
    for i in range(4):
        cs += [slot(ci, 1536 + 128 * i), slot(ci, 2048 + 128 * i), slot(ci, 1024 + 128 * i)]
    for ks in ([4, 5, 6, 7], [0, 1, 2, 3]):
        for m in range(4):
            cs.append(_tiles(co, [256 * m] * 4 + [256 * m + 128] * 4, ks + ks))
    w_cd = np.stack(cs + gate_up(1))

    x = a["x"][0].T.reshape(KD, 128, T).transpose(1, 0, 2)
    x_nat = np.ascontiguousarray(x)
    x_cls = np.ascontiguousarray(x.reshape(128, KD, 128, 4).transpose(0, 1, 3, 2).reshape(128, KD, T))

    def cols(vec):
        return vec.reshape(-1, 128).T

    qk = []
    for g in range(3):
        for n in ("q_norm_g", "k_norm_g"):
            qk.append(np.concatenate([a[n][0, g], a[n][0, g]])[:, None])

    def taps(w):
        return w.T.reshape(4, 128, w.shape[0]).transpose(1, 0, 2).reshape(128, -1)

    vecs = np.concatenate(qk + [cols(a["ab_norm_g"][0]), cols(a["ffn_norm_g"][0]), cols(a["cd_norm_g"][0]),
                                cols(a["ffn_norm_g"][1]), taps(a["conv_c_w"][0]), cols(a["conv_c_b"][0]),
                                cols(a["c_ln_g"][0]), cols(a["c_ln_b"][0]), taps(a["conv_d_w"][0]),
                           cols(a["sgu_norm_g"][0]), cols(a["sgu_norm_b"][0])], axis=1)
    sgu_bias = np.broadcast_to(a["sgu_bias"][0].reshape(1, 4, 128), (128, 4, 128))
    sguw = a["sgu_w"][0].transpose(2, 0, 1)

    consts = np.zeros((128, C_N), f)
    consts[:, C_ID:C_ID + 128] = np.eye(128, dtype=f)
    consts[0:64, C_HM] = 1 / 64
    consts[64:128, C_HM + 1] = 1 / 64
    consts[:, C_1024] = 1 / 1024
    consts[:, C_512] = 1 / 512
    consts[:, C_AVG:C_ONES] = 1 / 512
    consts[:, C_ONES:] = 1
    i = np.arange(128)
    masks = np.zeros((128, 4, KEYS), f)
    for r in range(4):
        tq = 4 * i + r
        for c in range(4):
            dist = tq[:, None] - (4 * i + c)[None, :]
            masks[:, r, 128 * c:128 * c + 128] = np.where((dist >= 0) & (dist <= 128), 0, -1e30)
        causal = i[:, None] >= i[None, :]
        masks[:, r, 512:640] = np.where(causal, 0, -1e30)
        masks[:, r, 640:768] = np.where(causal & ((i[:, None] - i[None, :]) % 4 == 0), 0, -1e30)
    inv = f(500000.0) ** (-np.arange(8, dtype=f) * f(2.0) / f(16))
    pos = (4 * i[None, :] + np.arange(4)[:, None]).reshape(-1).astype(f)
    ang = (pos[None, :] * inv.astype(f)[:, None]).astype(f)
    rope = np.zeros((128, 2, T), f)
    rope[:, 0, :] = 1
    for h in (0, 64):
        rope[h:h + 8, 0], rope[h + 8:h + 16, 0] = np.cos(ang), np.cos(ang)
        rope[h:h + 8, 1], rope[h + 8:h + 16, 1] = -np.sin(ang), np.sin(ang)

    arrays = {"x_cls": x_cls, "x_nat": x_nat, "w_ab": w_ab, "w_dn0": down(0), "w_cd": w_cd, "w_dn1": down(1),
              "vecs_d": vecs, "consts_d": consts, "sgu_bias_d": sgu_bias, "sguw_d": sguw, "masks_d": masks, "rope_d": rope}
    nc = _bacc.Bacc("TRN2", target_bir_lowering=False, num_devices=1)
    args = []
    for name in arrays:
        arrays[name] = np.ascontiguousarray(arrays[name])
        args.append(nc.dram_tensor(name, arrays[name].shape, _mybir.dt.float32, kind="ExternalInput").ap())
    out = nc.dram_tensor("out", [KD, 128, T], _mybir.dt.float32, kind="ExternalOutput").ap()
    build(nc, *args, out)
    r = _run(nc, [arrays], core_ids=[0])
    got = np.asarray(r.results[0]["out"])
    return np.ascontiguousarray(got.reshape(D, T).T).reshape(1, T, D)
```
